# Optimizing a Trainium2 kernel written in Bass

```python
import jax, jax.numpy as jnp
from jax import lax
import numpy as np

D_MODEL = 1024
BATCH = 1
SEQ = 512
DEPTH = 1

MIX_WIDTH = D_MODEL
RET_HEADS = 4
RET_DK = MIX_WIDTH // 2 // RET_HEADS
RET_DV = MIX_WIDTH // 2 // RET_HEADS
RET_CHUNK = 128
ATT_HEADS = 4
ATT_DH = MIX_WIDTH // 2 // ATT_HEADS
DILATED_CONFIGS = ((128, 1), (512, 4), (2048, 16))
ATT_BLOCK = 128
ROPE_THETA = 10000.0
N_EXPERTS = 32
TOP_K = 4
D_EXPERT = D_MODEL
SWIGLU_LIMIT = 7.0
SWIGLU_ALPHA = 1.702
MOE_BLOCK = 128
NORM_EPS = 1e-5
IN_SIZES = (RET_HEADS * RET_DK, RET_HEADS * RET_DK, RET_HEADS * RET_DV, RET_HEADS * RET_DV,
            ATT_HEADS * ATT_DH, ATT_HEADS * ATT_DH, ATT_HEADS * ATT_DH)
D_IN = sum(IN_SIZES)
D_CAT = RET_HEADS * RET_DV + ATT_HEADS * ATT_DH

kernel_name = "hybrid_retention_dilated_moe_block"

def rms_norm(x, g):
    xf = x.astype(jnp.float32)
    y = xf * lax.rsqrt(jnp.mean(xf * xf, axis=-1, keepdims=True) + NORM_EPS)
    return (y * g.astype(jnp.float32)).astype(x.dtype)

def rotary(t, pos):
    dh = t.shape[-1]
    inv = ROPE_THETA ** (-jnp.arange(0, dh, 2, dtype=jnp.float32) / dh)
    ang = pos[:, None] * inv[None, :]
    cos = jnp.cos(ang)[None, :, None, :].astype(t.dtype)
    sin = jnp.sin(ang)[None, :, None, :].astype(t.dtype)
    t1, t2 = t[..., : dh // 2], t[..., dh // 2:]
    return jnp.concatenate([t1 * cos - t2 * sin, t1 * sin + t2 * cos], axis=-1)

def retention_chunkwise(q, k, v):
    B, S, H, Dk = q.shape
    Dv = v.shape[-1]
    C = RET_CHUNK
    N = S // C
    log_g = jnp.log1p(-(2.0 ** (-5.0 - jnp.arange(H, dtype=jnp.float32))))
    idx = jnp.arange(C, dtype=jnp.float32)
    diff = idx[:, None] - idx[None, :]
    intra_decay = jnp.where(diff[None] >= 0, jnp.exp(jnp.maximum(diff, 0.0)[None] * log_g[:, None, None]), 0.0)
    zeta = jnp.exp((C - 1 - idx)[None, :] * log_g[:, None])
    xi = jnp.exp((idx + 1)[None, :] * log_g[:, None])
    chunk_decay = jnp.exp(C * log_g)
    dt = q.dtype
    qc = q.reshape(B, N, C, H, Dk)
    kc = k.reshape(B, N, C, H, Dk)
    vc = v.reshape(B, N, C, H, Dv)
    s = jnp.einsum('bnihd,bnjhd->bnhij', qc, kc) * intra_decay.astype(dt)[None, None]
    intra = jnp.einsum('bnhij,bnjhe->bnihe', s, vc)
    kv = jnp.einsum('bnjhd,bnjhe,hj->nbhde', kc, vc, zeta.astype(dt))
    dec = chunk_decay.astype(dt)[None, :, None, None]

    def step(state, kv_n):
        return state * dec + kv_n, state

    _, state_prev = lax.scan(step, jnp.zeros((B, H, Dk, Dv), dt), kv)
    cross = jnp.einsum('bnihd,nbhde,hi->bnihe', qc, state_prev, xi.astype(dt))
    return (intra + cross).reshape(B, S, H, Dv)

def head_group_norm(o):
    of = o.astype(jnp.float32)
    mu = jnp.mean(of, axis=-1, keepdims=True)
    var = jnp.mean(jnp.square(of - mu), axis=-1, keepdims=True)
    return ((of - mu) * lax.rsqrt(var + NORM_EPS)).astype(o.dtype)

def dilated_branch(q, k, v, window, dilation):
    B, S, H, Dh = q.shape
    n_back = window // dilation
    L = S // dilation
    nb = -(-L // ATT_BLOCK)
    Lp = nb * ATT_BLOCK

    def to_sub(t):
        t = t.reshape(B, L, dilation, H, Dh).transpose(0, 2, 3, 1, 4)
        t = jnp.pad(t, ((0, 0), (0, 0), (0, 0), (0, Lp - L), (0, 0)))
        return t.reshape(B, dilation, H, nb, ATT_BLOCK, Dh)

    qs, ks, vs = to_sub(q), to_sub(k), to_sub(v)

    def with_prev(t):
        prev = jnp.concatenate([jnp.zeros_like(t[:, :, :, :1]), t[:, :, :, :-1]], axis=3)
        return jnp.concatenate([prev, t], axis=4)

    kk, vv = with_prev(ks), with_prev(vs)
    s = jnp.einsum('brhnqc,brhnkc->brhnqk', qs, kk).astype(jnp.float32)
    qi = jnp.arange(ATT_BLOCK)[:, None]
    kj = jnp.arange(2 * ATT_BLOCK)[None, :]
    dist = qi + ATT_BLOCK - kj
    band = (dist >= 0) & (dist <= n_back)
    blk = jnp.arange(nb)[:, None, None]
    valid = band[None] & ((kj[None] >= ATT_BLOCK) | (blk > 0))
    s = jnp.where(valid, s, -jnp.inf)
    m = jnp.max(s, axis=-1, keepdims=True)
    p = jnp.exp(s - m)
    den = jnp.sum(p, axis=-1, keepdims=True)
    o = jnp.einsum('brhnqk,brhnkc->brhnqc', p.astype(v.dtype), vv) / den.astype(v.dtype)
    lse = (m + jnp.log(den))[..., 0]
    o = o.reshape(B, dilation, H, Lp, Dh)[:, :, :, :L].transpose(0, 3, 1, 2, 4).reshape(B, S, H, Dh)
    lse = lse.reshape(B, dilation, H, Lp)[:, :, :, :L].transpose(0, 3, 1, 2).reshape(B, S, H)
    return o, lse

def dilated_mixture(q, k, v):
    outs, lses = [], []
    for window, dilation in DILATED_CONFIGS:
        o, lse = dilated_branch(q, k, v, window, dilation)
        outs.append(o)
        lses.append(lse)
    w = jax.nn.softmax(jnp.stack(lses, axis=0), axis=0)
    o = jnp.stack(outs, axis=0)
    return jnp.sum(w.astype(q.dtype)[..., None] * o, axis=0)

def hybrid_mixer(h, w_in, w_out, pos):
    B, S, _ = h.shape
    proj = h @ w_in
    offsets = list(np.cumsum(IN_SIZES)[:-1])
    rq, rk, rv, rg, aq, ak, av = jnp.split(proj, offsets, axis=-1)
    rq = rotary(rq.reshape(B, S, RET_HEADS, RET_DK), pos)
    rk = rotary(rk.reshape(B, S, RET_HEADS, RET_DK), pos) * (RET_DK ** -0.5)
    rv = rv.reshape(B, S, RET_HEADS, RET_DV)
    ret = head_group_norm(retention_chunkwise(rq, rk, rv)).reshape(B, S, RET_HEADS * RET_DV)
    ret = jax.nn.silu(rg) * ret
    aq = rotary(aq.reshape(B, S, ATT_HEADS, ATT_DH), pos) * (ATT_DH ** -0.5)
    ak = rotary(ak.reshape(B, S, ATT_HEADS, ATT_DH), pos)
    av = av.reshape(B, S, ATT_HEADS, ATT_DH)
    att = dilated_mixture(aq, ak, av).reshape(B, S, ATT_HEADS * ATT_DH)
    return jnp.concatenate([ret, att], axis=-1) @ w_out

def clamped_swiglu_expert(xb, w_gu, b_gu, w_dn, b_dn):
    gu = xb @ w_gu + b_gu
    x_glu, x_lin = gu[..., :D_EXPERT], gu[..., D_EXPERT:]
    x_glu = jnp.minimum(x_glu, SWIGLU_LIMIT)
    x_lin = jnp.clip(x_lin, -SWIGLU_LIMIT, SWIGLU_LIMIT)
    act = x_glu * jax.nn.sigmoid(SWIGLU_ALPHA * x_glu) * (x_lin + 1.0)
    return act @ w_dn + b_dn

def moe_ffn(h, w_router, b_router, w_gate_up, b_gate_up, w_down, b_down):
    B, S, D = h.shape
    T = B * S
    ht = h.reshape(T, D)
    logits = (ht @ w_router + b_router).astype(jnp.float32)
    top_val, top_idx = lax.top_k(logits, TOP_K)
    gates = jax.nn.softmax(top_val, axis=-1).astype(h.dtype)
    A = T * TOP_K
    e_flat = top_idx.reshape(A).astype(jnp.int32)
    g_flat = gates.reshape(A)
    tok_flat = jnp.arange(A, dtype=jnp.int32) // TOP_K
    order = jnp.argsort(e_flat, stable=True)
    e_sorted = e_flat[order]
    counts = jnp.bincount(e_flat, length=N_EXPERTS)
    padded = (counts + MOE_BLOCK - 1) // MOE_BLOCK * MOE_BLOCK
    start = jnp.cumsum(counts) - counts
    pend = jnp.cumsum(padded)
    pstart = pend - padded
    dest = pstart[e_sorted] + (jnp.arange(A, dtype=jnp.int32) - start[e_sorted])
    P = A + N_EXPERTS * MOE_BLOCK
    n_blk = P // MOE_BLOCK
    rows_tok = jnp.zeros((P,), jnp.int32).at[dest].set(tok_flat[order])
    rows_gate = jnp.zeros((P,), h.dtype).at[dest].set(g_flat[order])
    blk_expert = jnp.minimum(
        jnp.searchsorted(pend, jnp.arange(n_blk, dtype=jnp.int32) * MOE_BLOCK, side='right'),
        N_EXPERTS - 1).astype(jnp.int32)
    xb = ht[rows_tok].reshape(n_blk, MOE_BLOCK, D)

    def run_block(args):
        xblk, e = args
        return clamped_swiglu_expert(xblk, w_gate_up[e], b_gate_up[e], w_down[e], b_down[e])

    yb = lax.map(run_block, (xb, blk_expert)).reshape(P, D)
    y = jnp.zeros((T, D), h.dtype).at[rows_tok].add(yb * rows_gate[:, None])
    return y.reshape(B, S, D)

def setup_inputs(seed: int = 0) -> dict:
    key = jax.random.key(seed)
    ks = jax.random.split(key, 12)
    f32 = jnp.float32
    nrm = lambda k, shape, scale: jax.random.normal(k, shape, f32) * scale
    return {
        "x": nrm(ks[0], (BATCH, SEQ, D_MODEL), 1.0),
        "norm_mix_g": 1.0 + nrm(ks[1], (DEPTH, D_MODEL), 0.02),
        "w_in": nrm(ks[2], (DEPTH, D_MODEL, D_IN), D_MODEL ** -0.5),
        "w_out": nrm(ks[3], (DEPTH, D_CAT, D_MODEL), D_CAT ** -0.5),
        "norm_ffn_g": 1.0 + nrm(ks[4], (DEPTH, D_MODEL), 0.02),
        "w_router": nrm(ks[5], (DEPTH, D_MODEL, N_EXPERTS), D_MODEL ** -0.5),
        "b_router": nrm(ks[6], (DEPTH, N_EXPERTS), 0.01),
        "w_gate_up": nrm(ks[7], (DEPTH, N_EXPERTS, D_MODEL, 2 * D_EXPERT), D_MODEL ** -0.5),
        "b_gate_up": nrm(ks[8], (DEPTH, N_EXPERTS, 2 * D_EXPERT), 0.01),
        "w_down": nrm(ks[9], (DEPTH, N_EXPERTS, D_EXPERT, D_MODEL), D_EXPERT ** -0.5),
        "b_down": nrm(ks[10], (DEPTH, N_EXPERTS, D_MODEL), 0.01),
        "norm_final_g": 1.0 + nrm(ks[11], (D_MODEL,), 0.02),
    }

def reference(x, norm_mix_g, w_in, w_out, norm_ffn_g, w_router, b_router,
              w_gate_up, b_gate_up, w_down, b_down, norm_final_g):
    S = x.shape[1]
    pos = jnp.arange(S, dtype=jnp.float32)
    for l in range(DEPTH):
        x = x + hybrid_mixer(rms_norm(x, norm_mix_g[l]), w_in[l], w_out[l], pos)
        x = x + moe_ffn(rms_norm(x, norm_ffn_g[l]), w_router[l], b_router[l],
                        w_gate_up[l], b_gate_up[l], w_down[l], b_down[l])
    return rms_norm(x, norm_final_g)


_drawn_inputs = setup_inputs


def setup_inputs(seed=0):
    import zlib

    import numpy as np

    out = dict(_drawn_inputs(seed))
    spreads = {}
    factors = {'b_gate_up': 8.0, 'b_down': 8.0, 'norm_final_g': 2.828}
    for name, (base, spread) in spreads.items():
        noise = np.random.default_rng([zlib.crc32(name.encode()), seed]).standard_normal(out[name].shape)
        drawn = base * np.exp(spread * noise) if base else spread * noise
        out[name] = __import__('jax').numpy.asarray(drawn.astype(out[name].dtype))
    for name, factor in factors.items():
        out[name] = (out[name] * factor).astype(out[name].dtype)
    return out
```

```python
import concourse.bass as bass
from concourse import mybir
import numpy as np

F32 = mybir.dt.float32
F32R = mybir.dt.float32r
U32 = mybir.dt.uint32
I32 = mybir.dt.int32
ALU = mybir.AluOpType
ACT = mybir.ActivationFunctionType
AX = mybir.AxisListType

P = 128
S = 512
D = 1024
NC = S // P
KD = D // P
H = 4
DH = 128
GW = H * DH
E = 32
TOPK = 4
EPS = 1e-5
LIMIT = 7.0
ALPHA = 1.702
SCALE = float(DH) ** -0.5
BIG_NEG = -1.0e30

KU = 4
UW = 512
UNIT = KU * UW
RAW = 4
SPLIT = 3
RQ, RK, RV, RG, AQ, AK, AV = range(7)
GROUPS = [AQ, AK, AV, RV, RQ, RK, RG]
NG = len(GROUPS)
RET = 8 * NG - 6
U_OUT = 2 * NG
U_MOE = U_OUT + 4
U_GU = 8
U_DN = 4
U_E = U_GU + U_DN
U_LOOP = U_MOE + U_GU
U_ALL = U_MOE + E * U_E
NOVER = 15
NBLK = S // P

C_ID = 0
C_TRI = C_ID + P
C_ONE = C_TRI + P
C_IOTA = C_ONE + P
C_TOK = C_IOTA + E
C_DEST = C_TOK + NC * TOPK
C_SEL = C_DEST + NC * TOPK
C_OVE = C_SEL + 40
C_OVC = C_OVE + 3 * E
C_NUM = C_OVC + 3 * E
C_SMALL = C_NUM + 16
M_COS = 0
M_SIN = M_COS + NC * DH
M_W = M_SIN + NC * DH
M_NEG = M_W + S
M_SMALL = M_NEG + S


def constants():
    small = np.zeros((P, C_SMALL), np.float32)
    p = np.arange(P)
    small[:, C_ID:C_ID + P] = np.eye(P)
    small[:, C_TRI:C_TRI + P] = (p[:, None] < p[None, :])
    small[:, C_ONE:C_ONE + P] = 1.0
    small[:, C_IOTA:C_IOTA + E] = np.arange(E)[None]
    ck = np.arange(NC * TOPK)
    small[:, C_TOK:C_TOK + NC * TOPK] = (ck // TOPK * P)[None] + p[:, None]
    small[:, C_DEST:C_DEST + NC * TOPK] = ((ck // TOPK * P)[None] + p[:, None]) * TOPK + ck % TOPK
    for e in range(E):
        small[e, C_SEL + e] = 1.0
        small[E + e, C_SEL + e] = 1.0
    pair = np.arange(3 * E)
    small[:, C_OVE:C_OVE + 3 * E] = (pair % E)[None]
    small[:, C_OVC:C_OVC + 3 * E] = (pair + E)[None]
    small[:, C_NUM:C_NUM + 16] = np.arange(1, 17)[None]

    mix = np.zeros((P, M_SMALL), np.float32)
    inv = np.float32(10000.0) ** (-np.arange(0, DH, 2, dtype=np.float32) / np.float32(DH))
    ang = np.arange(S, dtype=np.float32)[:, None] * inv[None, :]
    cos, sin = np.cos(ang), np.sin(ang)
    cc = np.concatenate([cos, cos], 1).reshape(NC, P, DH).transpose(1, 0, 2)
    ss = np.concatenate([-sin, sin], 1).reshape(NC, P, DH).transpose(1, 0, 2)
    mix[:, M_COS:M_COS + NC * DH] = cc.reshape(P, -1)
    mix[:, M_SIN:M_SIN + NC * DH] = ss.reshape(P, -1)
    dist = (NC - 1) * P + p[:, None] - np.arange(S)[None, :]
    w = np.zeros((P, S), np.float32)
    for window, dil in ((128, 1), (512, 4), (2048, 16)):
        w += (dist >= 0) & (dist % dil == 0) & (dist // dil <= window // dil)
    mix[:, M_W:M_W + S] = w
    mix[:, M_NEG:M_NEG + S] = np.where(w > 0, 0.0, BIG_NEG)

    m = np.arange(S)[None, :] - p[:, None]
    log_g = np.log1p(-(2.0 ** (-5.0 - np.arange(H, dtype=np.float64))))
    dec = np.where(m[None] >= 0, np.exp(np.maximum(m, 0)[None] * log_g[:, None, None]), 0.0) * DH ** -0.5
    decay = dec.transpose(1, 0, 2).reshape(P, H * S).astype(np.float32)
    empty = np.zeros((P, NBLK * E, 4), np.uint32)
    empty[:, :, 0:2] = 4096
    return small, mix, decay, empty.reshape(P, -1)


def build(nc, x, norm_mix_g, w_in, w_out, norm_ffn_g, w_router, b_router,
          w_gate_up, b_gate_up, w_down, b_down, norm_final_g, out):
    small_np, mix_np, decay_np, empty_np = constants()
    small_d = nc.inline_tensor(small_np, name="const_small").ap()
    mix_d = nc.inline_tensor(mix_np, name="const_mix").ap()
    decay_d = nc.inline_tensor(decay_np, name="const_decay").ap()
    empty_d = nc.inline_tensor(empty_np, name="const_empty").ap()
    h_rows = nc.dram_tensor("h_rows", [S, D], F32).ap()
    table_d = nc.dram_tensor("slot_table", [S * E, 4], U32).ap()
    y_rows = nc.dram_tensor("y_rows", [S * TOPK, D], F32).ap()

    def place(offset, name, cols, dt=F32):
        t = nc.alloc_sbuf_tensor_at(name, [P, *cols], dt, offset=offset)
        return t, (offset + int(np.prod(cols)) * 4 + 31) // 32 * 32

    base = (nc.sbuf_base + 63) // 64 * 64
    raw, o = place(base, "raw", [RAW, UNIT])
    whi, o = place(o, "whi", [SPLIT, UNIT], F32R)
    wlo, o = place(o, "wlo", [SPLIT, UNIT], F32R)
    x1, o = place(o, "x1", [NC, D])
    cst, o = place(o, "cst", [C_SMALL])
    gmix, o = place(o, "gmix", [KD])
    small, o = place(o, "small", [16, 16])
    mv, o = place(o, "mv", [NC * H, 2])
    stats6, o = place(o, "stats6", [NC * H, 6])
    ov_lists, o = place(o, "ov_lists", [2, 16], I32)
    ov_total, o = place(o, "ov_total", [2], I32)
    idx_gather, o = place(o, "idx_gather", [1], U32)
    idx_scatter, o = place(o, "idx_scatter", [1], U32)
    area = (o + 63) // 64 * 64
    K = 1024
    hT_hi, _ = place(area, "hT_hi", [KD, S], F32R)
    hT_lo, _ = place(area + 16 * K, "hT_lo", [KD, S], F32R)
    qT, _ = place(area + 32 * K, "qT", [H, S])
    kT, _ = place(area + 40 * K, "kT", [H, S])
    avt, _ = place(area + 48 * K, "avt", [NC, GW])
    rvt, _ = place(area + 56 * K, "rvt", [NC, GW])
    rgt, _ = place(area + 64 * K, "rgt", [NC, GW])
    cat_att, _ = place(area + 72 * K, "cat_att", [NC, GW])
    rot, _ = place(area + 80 * K, "rot", [2, GW])
    rtmp, _ = place(area + 84 * K, "rtmp", [GW])
    prob, _ = place(area + 86 * K, "prob", [3, S])
    probT, _ = place(area + 92 * K, "probT", [S])
    mix, o = place(area + 94 * K, "mix", [M_SMALL])
    assert o <= nc.sbuf_usable_end, (o, nc.sbuf_usable_end)
    xn, _ = place(area + 32 * K, "xn", [NC, D])
    catT_hi, _ = place(area, "catT_hi", [KD, S], F32R)
    catT_lo, _ = place(area + 16 * K, "catT_lo", [KD, S], F32R)
    cat_ret, _ = place(area + 48 * K, "cat_ret", [NC, GW])
    st0, _ = place(area + 86 * K, "st0", [1280])
    st1, _ = place(area + 80 * K, "st1", [1280])
    decay23, _ = place(area + 94 * K, "decay23", [2, S])
    decay01, _ = place(area + 98 * K, "decay01", [2, S])
    hnT, _ = place(area, "hnT", [KD, S])
    hn, _ = place(area + 32 * K, "hn", [NC, D])
    g_row, _ = place(area + 64 * K, "g_row", [D])
    wr, o = place(area + 72 * K, "wr", [KD, E])
    br, o = place(o, "br", [E])
    logits, o = place(o, "logits", [NC, E])
    onehot, o = place(o, "onehot", [NC * TOPK, E])
    masks, o = place(o, "masks", [NC, E])
    prod, o = place(o, "prod", [NC * TOPK, E])
    top8, o = place(o, "top8", [NC, 8])
    idx8, o = place(o, "idx8", [NC, 8], U32)
    idxf, o = place(o, "idxf", [NC * TOPK])
    posk, o = place(o, "posk", [NC * TOPK])
    rowf, o = place(o, "rowf", [NC * TOPK])
    gates, o = place(o, "gates", [NC, TOPK])
    assert o <= area + 80 * K
    row_idx, o = place(area + 68 * K, "row_idx", [NC * TOPK], U32)
    rows, o = place(o, "rows", [NC * TOPK, 4], U32)
    counts, o = place(o, "counts", [E])
    ovf, o = place(o, "ovf", [3 * E])
    ovr, o = place(o, "ovr", [3 * E])
    ovt, o = place(o, "ovt", [3 * E])
    ov_out, o = place(o, "ov_out", [2, 16])
    assert o <= area + 72 * K
    ov_eq, _ = place(area + 80 * K, "ov_eq", [16, 3 * E])
    tab, _ = place(area + 16 * K, "tab", [NBLK * E, 4], U32)
    xT_hi, _ = place(area + 24 * K, "xT_hi", [KD, P], F32R)
    xT_lo, _ = place(area + 28 * K, "xT_lo", [KD, P], F32R)
    bias_raw, _ = place(area + 32 * K, "bias_raw", [3 * D])
    xg, _ = place(area + 48 * K, "xg", [D])
    act, _ = place(area + 52 * K, "act", [D])
    actT_hi, _ = place(area + 56 * K, "actT_hi", [KD, P], F32R)
    actT_lo, _ = place(area + 60 * K, "actT_lo", [KD, P], F32R)
    y, _ = place(area + 72 * K, "y", [D])
    glu, o = place(area + 76 * K, "glu", [UW])
    lin, o = place(o, "lin", [UW])
    bias, _ = place(area + 80 * K, "bias", [3 * D], F32R)
    sig, o = place(area + 92 * K, "sig", [UW])
    sel_gu, o = place(o, "sel_gu", [P], F32R)
    sel_dn, o = place(o, "sel_dn", [P], F32R)
    xT32, _ = place(area + 24 * K, "xT32", [KD, P])
    actT32, _ = place(area + 56 * K, "actT32", [KD, P])
    selv, _ = place(area + 95 * K, "selv", [P])
    bias32 = bias
    picked = [place(at, f"picked{c}", [TOPK, D])[0] for c, at in enumerate((area, area + 32 * K, base, base + 16 * K))]

    ps = nc.alloc_psum_tensor("ps", [P, 8, UW], F32)

    ident = cst[:, C_ID:C_ID + P]
    ones = cst[:, C_ONE:C_ONE + P]

    def sem(name):
        return nc.alloc_semaphore(name)

    raw_full = [sem(f"raw_full{r}") for r in range(RAW)]
    hi_done, lo_done = sem("hi_done"), sem("lo_done")
    used = sem("units_used")
    x_in = [sem(f"x_in{c}") for c in range(NC)]
    cst_in, mix_in, gmix_in = sem("cst_in"), sem("mix_in"), sem("gmix_in")
    table_empty = sem("table_empty")
    sq, var_s, root_s, rstd_s = sem("squares"), sem("variance"), sem("root"), sem("rstd")
    xn_s, xT_tr = sem("xn_ready"), sem("xn_transposed")
    hThi_s, hTlo_s = sem("hT_hi_ready"), sem("hT_lo_ready")
    dve = sem("vector_chain")
    proj = sem("projected")
    drained_v, drained_s = sem("drained_by_vector"), sem("drained_by_scalar")
    rot_s, rot_tr, rot_out = sem("rotated"), sem("rot_transposed"), sem("rot_stored")
    a_score, a_max, a_exp, a_prob = sem("att_scores"), sem("att_max"), sem("att_exp"), sem("att_prob")
    a_tr, a_pT, a_pv, a_out = sem("att_transposed"), sem("att_probT"), sem("att_pv"), sem("att_out")
    dec01_in, dec23_in = sem("decay01_in"), sem("decay23_in")
    r_score, r_st, r_pv, r_copy = sem("ret_scores"), sem("ret_decayed"), sem("ret_pv"), sem("ret_copied")
    g_sig, g_use, g_gate, r_cat = sem("gate_sigmoid"), sem("gate_used"), sem("gate_ready"), sem("ret_ready")
    gn_var, gn_root = sem("group_variance"), sem("group_root")
    c_tr, c_hi, c_lo = sem("cat_transposed"), sem("cat_hi"), sem("cat_lo")
    x1_s = sem("residual_added")
    ffn_g_in, router_in = sem("ffn_gain_in"), sem("router_in")
    hn_s, hn_out, hn_tr, hnT_s = sem("hn_ready"), sem("hn_stored"), sem("hn_transposed"), sem("hnT_ready")
    logit_s, mask_s, pos_s = sem("logits_ready"), sem("masks_ready"), sem("positions_ready")
    top_s, gexp_s, rows_s, rows_out, tab_in = (sem("top_ready"), sem("gate_exp"), sem("rows_ready"),
                                               sem("rows_stored"), sem("table_in"))
    a_read, a_rden = sem("att_scores_read"), sem("att_row_sums")
    v_chain = sem("over_vector_chain")
    bias_in, bias_s, ov_s = sem("bias_in"), sem("bias_ready"), sem("overflow_listed")
    pool = sem("pool_chain")
    sel_gu_s, sel_dn_s = sem("select_gate_up"), sem("select_down")
    gathered, scattered = sem("gathered"), sem("scattered")
    x_tr, x_hi, x_lo = sem("tokens_transposed"), sem("tokens_hi"), sem("tokens_lo")
    glu_s, lin_s, gated_s, sig_s, act_s = (sem("glu_clamped"), sem("lin_clamped"), sem("gated"),
                                           sem("sigmoid_ready"), sem("act_ready"))
    act_tr, aT_hi, aT_lo = sem("act_transposed"), sem("actT_hi"), sem("actT_lo")
    y_s, y_free = sem("y_ready"), sem("y_free")
    fin_g_in, rows_done = sem("final_gain_in"), sem("all_rows_stored")
    picked_in = [sem(f"picked_in{c}") for c in range(NC)]
    f_sum, f_sq, f_var, f_root, f_out, stored = (sem("final_sum"), sem("final_squares"), sem("final_variance"),
                                         sem("final_root"), sem("final_rows"), sem("outputs_stored"))
    v_full = [sem(f"over_raw_full{r}") for r in range(RAW)]
    v_free, v_sel, v_gather, v_tr, v_xT, v_sig, v_act, v_aT, v_y, v_scatter, v_mid = (
        sem("over_raw_free"), sem("over_select"), sem("over_gathered"), sem("over_transposed"),
        sem("over_tokens"), sem("over_sigmoid"), sem("over_act"), sem("over_actT"),
        sem("over_y"), sem("over_scattered"), sem("over_glu"))

    win_v = w_in[0].rearrange("(k p) (g c) -> p g k c", p=P, c=UW)
    wout_v = w_out[0].rearrange("(k p) (g c) -> p g k c", p=P, c=UW)
    wgu_v = w_gate_up[0].rearrange("e (k p) (g c) -> p e g k c", p=P, c=UW)
    wdn_v = w_down[0].rearrange("e (k p) (g c) -> p e g k c", p=P, c=UW)

    def mixer_source(n):
        if n < U_OUT:
            return win_v[:, GROUPS[n // 2], KU * (n % 2):KU * (n % 2) + KU, :]
        g, part = divmod(n - U_OUT, 2)
        return wout_v[:, g, KU * (1 - part):KU * (1 - part) + KU, :]

    GU_COLS = [0, 2, 1, 3]

    def raw4(r):
        return raw[:, r, :].rearrange("p (k c) -> p k c", k=KU)

    def wait_bank(eng, g, c):
        if c < NC - 1:
            eng.wait_ge(proj, (NC - 1) * g + c + 1)
        else:
            eng.wait_ge(used, 2 * g + 2)

    block = nc.Block()
    with block as block:
        @block.sync
        def _(sp):
            def load(n, i, source):
                if n >= RAW:
                    sp.wait_ge(lo_done, i * U_E + (n - RAW + 1))
                sp.dma_start(raw4(n % RAW), source).then_inc(raw_full[n % RAW], 16)

            for c in range(NC):
                sp.dma_start(x1[:, c, :], x[0, c * P:(c + 1) * P, :]).then_inc(x_in[c], 16)
            for n in range(U_LOOP):
                if n == U_MOE + RAW:
                    for c in range(NC):
                        sp.wait_ge(hn_s, c + 1)
                        sp.dma_start(h_rows[c * P:(c + 1) * P, :], hn[:, c, :]).then_inc(hn_out, 16)
                if n < U_MOE:
                    load(n, 0, mixer_source(n))
                else:
                    u = n - U_MOE
                    load(n, 0, wgu_v[:, 0, GU_COLS[u // 2], KU * (u % 2):KU * (u % 2) + KU, :])
            with sp.Fori(0, E - 1) as i:
                for u in range(U_E):
                    k0 = KU * (u % 2)
                    if u < U_GU:
                        src = wgu_v[:, bass.ds(i + 1, 1), GU_COLS[u // 2], k0:k0 + KU, :]
                    else:
                        src = wdn_v[:, bass.ds(i, 1), (u - U_GU) // 2, k0:k0 + KU, :]
                    load(U_LOOP + u, i, src.rearrange("p e k c -> p (e k) c"))
            for u in range(U_DN):
                load(U_ALL - U_DN + u, 0, wdn_v[:, E - 1, u // 2, KU * (u % 2):KU * (u % 2) + KU, :])

            sp.wait_ge(ov_s, 1)
            sp.wait_ge(lo_done, U_ALL)
            total = sp.value_load(ov_total[0:1, 0:1], min_val=0, max_val=NOVER)
            with sp.If(total > 0):
                with sp.Fori(0, NOVER) as i:
                    with sp.If(i < total):
                        e = sp.value_load(ov_lists[0:1, 0, bass.ds(i, 1)], min_val=0, max_val=E - 1)
                        for u in range(U_E):
                            k0 = KU * (u % 2)
                            sp.wait_ge(v_free, i * U_E + (u + 1))
                            if u < U_GU:
                                src = wgu_v[:, bass.ds(e, 1), GU_COLS[u // 2], k0:k0 + KU, :]
                            else:
                                src = wdn_v[:, bass.ds(e, 1), (u - U_GU) // 2, k0:k0 + KU, :]
                            sp.dma_start(raw4(u % RAW), src.rearrange("p e k c -> p (e k) c")).then_inc(v_full[u % RAW], 16)

            sp.wait_ge(rows_done, 1)
            y_view = y_rows.rearrange("(c p k) d -> c p k d", p=P, k=TOPK)
            for c in range(NC):
                sp.dma_start(picked[c][:, :, :], y_view[c]).then_inc(picked_in[c], 16)
            for c in range(NC):
                sp.wait_ge(f_out, c + 1)
                sp.dma_start(out[0, c * P:(c + 1) * P, :], x1[:, c, :]).then_inc(stored, 16)
            sp.wait_ge(stored, 16 * NC)

        @block.gpsimd
        def _(pl):
            chain = [0]

            def link(ins):
                chain[0] += 1
                ins.then_inc(pool, 1)
                pl.wait_ge(pool, chain[0])

            pl.dma_start(table_d.rearrange("(p r) f -> p (r f)", p=P), empty_d).then_inc(table_empty, 16)
            pl.wait_ge(a_prob, NC * H)
            pl.dma_start(decay01[:, :, :], decay_d[:, 0:2 * S].rearrange("p (h m) -> p h m", h=2)).then_inc(dec01_in, 16)
            pl.wait_ge(rot_s, 16)
            pl.dma_start(decay23[:, :, :], decay_d[:, 2 * S:4 * S].rearrange("p (h m) -> p h m", h=2)).then_inc(dec23_in, 16)
            pl.wait_ge(c_tr, H)
            link(nc.gpsimd.memset(br[:, :], 0.0))
            with nc.allow_non_contiguous_dma(reason="rows of 128 bytes"):
                pl.dma_start(wr[:, :, :], w_router[0].rearrange("(k p) e -> p k e", p=P)).then_inc(router_in, 16)
                pl.dma_start(br[0:1, :], b_router[0:1, :]).then_inc(router_in, 16)
            pl.wait_ge(r_cat, H)
            pl.dma_start(g_row[:, :], norm_ffn_g[0:1, :].to_broadcast([P, D])).then_inc(ffn_g_in, 16)
            pl.wait_ge(c_tr, 2 * H)
            link(nc.gpsimd.memset(xg[:, :], 0.0))
            pl.wait_ge(hn_tr, KD)
            pl.wait_ge(hn_out, 16 * NC)
            link(nc.gpsimd.memset(bias[2 * E:P, :].bitcast(F32), 0.0))
            for r in (0, E):
                pl.dma_start(bias_raw[r:r + E, 0:2 * D], b_gate_up[0]).then_inc(bias_in, 16)
                pl.dma_start(bias_raw[r:r + E, 2 * D:3 * D], b_down[0]).then_inc(bias_in, 16)
            pl.dma_start(g_row[:, :], norm_final_g.rearrange("(o d) -> o d", o=1).to_broadcast([P, D])).then_inc(fin_g_in, 16)

            pl.wait_ge(table_empty, 16)
            pl.wait_ge(rows_s, 1)
            for j in range(NC * TOPK):
                pl.indirect_dma_start(out=table_d, out_offset=bass.IndirectOffsetOnAxis(ap=row_idx[:, j:j + 1], axis=0),
                                      in_=rows[:, j, :], in_offset=None).then_inc(rows_out, 16)
            pl.wait_ge(rows_out, 16 * NC * TOPK)
            pl.dma_start(tab[:, :, :].rearrange("p (b e) f -> p b (e f)", b=NBLK),
                         table_d.rearrange("(b p e) f -> p b (e f)", b=NBLK, p=P)).then_inc(tab_in, 16)
            pl.wait_ge(tab_in, 16)

            def gather(column, done):
                nc.gpsimd.tensor_copy(idx_gather[:, 0:1], tab[:, bass.ds(column, 1), 0])
                pl.drain()
                pl.indirect_dma_start(out=xg[:, :], out_offset=None, in_=h_rows,
                                      in_offset=bass.IndirectOffsetOnAxis(ap=idx_gather[:, 0:1], axis=0),
                                      bounds_check=S - 1, oob_is_err=False).then_inc(done, 16)

            def scatter(column, done):
                nc.gpsimd.tensor_copy(idx_scatter[:, 0:1], tab[:, bass.ds(column, 1), 1])
                pl.drain()
                pl.indirect_dma_start(out=y_rows, out_offset=bass.IndirectOffsetOnAxis(ap=idx_scatter[:, 0:1], axis=0),
                                      in_=y[:, :], in_offset=None,
                                      bounds_check=S * TOPK - 1, oob_is_err=False).then_inc(done, 16)

            def select(tile, column):
                return nc.gpsimd.tensor_copy(tile[:, :], cst[:, bass.ds(C_SEL + column, 1)].to_broadcast([P, P]))

            gather(0, gathered)
            pl.wait_ge(cst_in, 16)
            select(sel_gu, 0).then_inc(sel_gu_s, 1)
            pl.wait_ge(x_tr, 1)
            gather(1, gathered)
            pl.wait_ge(used, U_LOOP)
            select(sel_gu, 1).then_inc(sel_gu_s, 1)
            select(sel_dn, 0).then_inc(sel_dn_s, 1)
            pl.sem_inc(y_free, 1)
            with pl.Fori(0, E - 1) as i:
                pl.wait_ge(x_tr, i + 2)
                pl.wait_ge(gathered, i * 16 + 32)
                gather(i + 2, gathered)
                pl.wait_ge(used, i * U_E + (U_LOOP + U_GU))
                select(sel_gu, i + 2).then_inc(sel_gu_s, 1)
                pl.wait_ge(used, i * U_E + (U_LOOP + U_E))
                select(sel_dn, i + 1).then_inc(sel_dn_s, 1)
                pl.wait_ge(y_s, i + 2)
                scatter(i, scattered)
                pl.wait_ge(scattered, i * 16 + 16)
                pl.sem_inc(y_free, 1)
            pl.wait_ge(y_s, E + 1)
            scatter(E - 1, scattered)
            pl.wait_ge(scattered, 16 * E)
            pl.wait_ge(x_tr, E + 1)
            pl.wait_ge(gathered, 16 * (E + 1))

            pl.wait_ge(ov_s, 1)
            total = pl.value_load(ov_total[0:1, 0:1], min_val=0, max_val=NOVER)
            with pl.If(total > 0):
                with pl.Fori(0, NOVER) as i:
                    with pl.If(i < total):
                        e = pl.value_load(ov_lists[0:1, 0, bass.ds(i, 1)], min_val=0, max_val=E - 1)
                        column = pl.value_load(ov_lists[0:1, 1, bass.ds(i, 1)], min_val=0, max_val=NBLK * E - 1)
                        select(sel_gu, e).then_inc(v_sel, 1)
                        gather(column, v_gather)
                        pl.wait_ge(v_y, i + 1)
                        scatter(column, v_scatter)
                        pl.wait_ge(v_scatter, i * 16 + 16)
            pl.sem_inc(rows_done, 1)

        @block.scalar
        def _(act_e):
            def hi(n, i=0):
                act_e.wait_ge(raw_full[n % RAW], i * (16 * U_E // RAW) + 16 * (n // RAW + 1))
                if n >= SPLIT:
                    act_e.wait_ge(used, i * U_E + (n - SPLIT + 1))
                nc.scalar.activation(whi[:, n % SPLIT, :], raw[:, n % RAW, :], ACT.Copy).then_inc(hi_done, 1)

            def store_rot(q):
                act_e.wait_ge(rot_tr, q + 1)
                dst = (qT, kT)[(q // NC) % 2]
                c = q % NC
                nc.scalar.activation(dst[:, :, c * P:(c + 1) * P],
                                     ps[:, 4 + q % 2, :].rearrange("p (h t) -> p h t", h=H), ACT.Copy).then_inc(rot_out, 1)

            act_e.dma_start(cst[:, :], small_d).then_inc(cst_in, 16)
            with nc.allow_non_contiguous_dma(reason="1024 gains, one for each feature, onto partitions"):
                act_e.dma_start(gmix[:, :], norm_mix_g[0].rearrange("(k p) -> p k", p=P)).then_inc(gmix_in, 16)
            act_e.dma_start(mix[:, :], mix_d).then_inc(mix_in, 16)
            for c in range(NC):
                act_e.wait_ge(x_in[c], 16)
                nc.scalar.activation(xn[:, c, :], x1[:, c, :], ACT.Square,
                                     accum_out=small[:, 0, c:c + 1]).then_inc(sq, 1)
            act_e.wait_ge(var_s, 1)
            nc.scalar.activation(small[:, 2, 0:NC], small[:, 1, 0:NC], ACT.Sqrt).then_inc(root_s, 1)
            hi(0)
            hi(1)
            act_e.wait_ge(gmix_in, 16)
            for j in range(KD):
                act_e.wait_ge(xT_tr, j + 1)
                nc.scalar.activation(hT_hi[:, j, :], ps[:, 4 + j % 4, :], ACT.Copy,
                                     scale=gmix[:, j:j + 1]).then_inc(hThi_s, 1)

            copied = {AV: avt, RG: rgt, RV: rvt}
            n_rot = 0
            for b in range(8 * NG):
                n, c = divmod(b, NC)
                gi, u = divmod(n, 2)
                if c == 0:
                    hi(n + 2)
                if RET + 2 <= b < RET + 2 + H:
                    act_e.wait_ge(r_pv, b - RET - 1)
                    h = b - RET - 2
                    nc.scalar.activation(cat_ret[:, :, h * DH:(h + 1) * DH],
                                         ps[:, 7, :].rearrange("p (c d) -> p c d", c=NC), ACT.Copy).then_inc(r_copy, 1)
                if u == 1 and GROUPS[gi] in copied:
                    wait_bank(act_e, gi, c)
                    nc.scalar.activation(copied[GROUPS[gi]][:, c, :], ps[:, c, :], ACT.Copy).then_inc(drained_s, 1)
                if 24 <= b < 24 + NC * H:
                    j = b - 24
                    act_e.wait_ge(a_pv, j + 1)
                    act_e.wait_ge(a_rden, j + 1)
                    nc.scalar.activation(cat_att[:, j % NC, (j // NC) * DH:(j // NC + 1) * DH], ps[:, 7, 0:DH],
                                         ACT.Copy, scale=small[:, 7, j:j + 1]).then_inc(a_out, 1)
                if 20 <= b < 20 + NC * H:
                    j = b - 20
                    kw = (j % NC + 1) * P
                    act_e.wait_ge(a_max, j + 1)
                    nc.scalar.activation(prob[:, j % 3, 0:kw], prob[:, j % 3, 0:kw], ACT.Exp, scale=SCALE,
                                         bias=small[:, 5, j:j + 1]).then_inc(a_exp, 1)
                if 22 <= b < 22 + NC * H:
                    j = b - 22
                    kw = (j % NC + 1) * P
                    act_e.wait_ge(a_tr, j + 1)
                    if j:
                        act_e.wait_ge(a_pv, j)
                    nc.scalar.activation(probT[:, 0:kw], ps[:, 6, 0:kw], ACT.Copy).then_inc(a_pT, 1)
                if u == 1 and GROUPS[gi] == RG:
                    act_e.wait_ge(drained_s, 2 * NC + c + 1)
                    act_e.wait_ge(a_pv, NC * H)
                    if c:
                        act_e.wait_ge(g_use, c)
                    nc.scalar.activation(probT[:, :], rgt[:, c, :], ACT.Sigmoid).then_inc(g_sig, 1)
                rb = b - 2
                if rb >= 0 and (rb // NC) % 2 == 1 and GROUPS[rb // 8] in (AQ, AK, RQ, RK):
                    store_rot(n_rot)
                    n_rot += 1
            for h in range(H):
                act_e.wait_ge(c_tr, h + 1)
                nc.scalar.activation(catT_hi[:, H + h, :], ps[:, 6 + h % 2, :], ACT.Copy).then_inc(c_hi, 1)
            hi(16)
            act_e.wait_ge(gn_var, 1)
            nc.scalar.activation(small[:, 9, :], small[:, 8, :], ACT.Sqrt).then_inc(gn_root, 1)
            for h in range(H):
                act_e.wait_ge(c_tr, H + h + 1)
                nc.scalar.activation(catT_hi[:, h, :], ps[:, 4 + h % 2, :], ACT.Copy).then_inc(c_hi, 1)
            hi(17)
            hi(18)
            hi(19)
            for c in range(NC):
                act_e.wait_ge(x1_s, NC + c + 1)
                nc.scalar.activation(hn[:, c, :], x1[:, c, :], ACT.Square,
                                     accum_out=small[:, 0, c:c + 1]).then_inc(sq, 1)
            act_e.wait_ge(var_s, 2)
            nc.scalar.activation(small[:, 2, 0:NC], small[:, 1, 0:NC], ACT.Sqrt).then_inc(root_s, 1)
            hi(20)
            for j in range(KD):
                act_e.wait_ge(hn_tr, j + 1)
                nc.scalar.activation(hnT[:, j, :], ps[:, 4 + j % 4, :], ACT.Copy).then_inc(hnT_s, 1)
            act_e.wait_ge(top_s, 1)
            nc.scalar.activation(gates[:, :, :], gates[:, :, :], ACT.Exp).then_inc(gexp_s, 1)

            def sigmoid(hn0, i=0):
                act_e.wait_ge(glu_s, i * 2 + (hn0 + 1))
                if hn0 > 0:
                    act_e.wait_ge(act_s, i * 2 + hn0)
                nc.scalar.activation(sig[:, :], glu[:, :], ACT.Sigmoid, scale=ALPHA).then_inc(sig_s, 1)

            def tokens_hi(e, i=0):
                act_e.wait_ge(x_tr, i + (e + 1))
                nc.scalar.activation(xT_hi[:, :, :].rearrange("p k t -> p (k t)"),
                                     ps[:, 6:8, :].rearrange("p b t -> p (b t)"), ACT.Copy).then_inc(x_hi, 1)

            def features_hi(e, i=0):
                act_e.wait_ge(act_tr, i + (e + 1))
                nc.scalar.activation(actT_hi[:, :, :].rearrange("p k t -> p (k t)"),
                                     ps[:, 6:8, :].rearrange("p b t -> p (b t)"), ACT.Copy).then_inc(aT_hi, 1)

            def gated_rows(column, frees, units):
                act_e.wait_ge(used, units)
                act_e.wait_ge(y_free, frees)
                nc.scalar.activation(y[:, :], ps[:, 4:6, :].rearrange("p b t -> p (b t)"), ACT.Copy,
                                     scale=tab[:, bass.ds(column, 1), 2].bitcast(F32)).then_inc(y_s, 1)

            act_e.sem_inc(y_s, 1)
            act_e.wait_ge(tab_in, 16)
            tokens_hi(0)
            for n in (21, 22, 23, 24, 25):
                hi(n)
            sigmoid(0)
            for n in (26, 27, 28):
                hi(n)
            tokens_hi(1)
            sigmoid(1)
            features_hi(0)
            with act_e.Fori(0, E - 1) as i:
                for n in (29, 30, 31, 32, 33):
                    hi(n, i)
                sigmoid(2, i)
                for n in (34, 35, 36):
                    hi(n, i)
                tokens_hi(2, i)
                hi(37, i)
                sigmoid(3, i)
                for n in (38, 39, 40):
                    hi(n, i)
                gated_rows(i, i + 1, i * U_E + (U_LOOP + U_E))
                features_hi(1, i)
            hi(U_ALL - 1)
            gated_rows(E - 1, E, U_ALL)

            act_e.wait_ge(ov_s, 1)
            total = act_e.value_load(ov_total[0:1, 0:1], min_val=0, max_val=NOVER)
            with act_e.If(total > 0):
                with act_e.Fori(0, NOVER) as i:
                    with act_e.If(i < total):
                        column = act_e.value_load(ov_lists[0:1, 1, bass.ds(i, 1)], min_val=0, max_val=NBLK * E - 1)
                        for half in range(2):
                            act_e.wait_ge(v_mid, i * 2 + (half + 1))
                            nc.scalar.activation(sig[:, :], glu[:, :], ACT.Sigmoid, scale=ALPHA).then_inc(v_sig, 1)
                        act_e.wait_ge(v_free, i * U_E + (RAW + U_E))
                        nc.scalar.activation(y[:, :], ps[:, 4:6, :].rearrange("p b t -> p (b t)"), ACT.Copy,
                                             scale=tab[:, bass.ds(column, 1), 2].bitcast(F32)).then_inc(v_y, 1)

            for c in range(NC):
                act_e.wait_ge(f_sum, c + 1)
                nc.scalar.activation(act[:, :], x1[:, c, :], ACT.Square,
                                     accum_out=small[:, 10, c:c + 1]).then_inc(f_sq, 1)
                act_e.wait_ge(f_var, c + 1)
                nc.scalar.activation(small[:, 12, c:c + 1], small[:, 11, c:c + 1], ACT.Sqrt).then_inc(f_root, 1)

        @block.vector
        def _(v):
            chain = [0]

            def link(ins):
                chain[0] += 1
                ins.then_inc(dve, 1)
                v.wait_ge(dve, chain[0])

            def lo(n, i=0):
                v.wait_ge(hi_done, i * U_E + (n + 1))
                nc.vector.tensor_tensor(wlo[:, n % SPLIT, :], raw[:, n % RAW, :],
                                        whi[:, n % SPLIT, :].bitcast(F32), ALU.subtract).then_inc(lo_done, 1)

            def inverse_root(var, root, r, t):
                link(nc.vector.reciprocal(r, root))
                link(nc.vector.tensor_tensor(t, r, r, ALU.mult))
                link(nc.vector.tensor_tensor(t, t, var, ALU.mult))
                link(nc.vector.tensor_scalar(t, t, -0.5, 1.5, ALU.mult, ALU.add))
                link(nc.vector.tensor_tensor(r, r, t, ALU.mult))

            v.wait_ge(sq, NC)
            nc.vector.tensor_scalar(small[:, 1, 0:NC], small[:, 0, 0:NC], 1.0 / D, EPS, ALU.mult, ALU.add).then_inc(var_s, 1)
            v.wait_ge(var_s, 1)
            v.wait_ge(root_s, 1)
            inverse_root(small[:, 1, 0:NC], small[:, 2, 0:NC], small[:, 3, 0:NC], small[:, 13, 0:NC])
            for c in range(NC):
                nc.vector.tensor_scalar(xn[:, c, :], x1[:, c, :], small[:, 3, c:c + 1], None, ALU.mult).then_inc(xn_s, 1)
            lo(0)
            lo(1)
            v.wait_ge(gmix_in, 16)
            for j in range(KD):
                v.wait_ge(hThi_s, j + 1)
                nc.vector.scalar_tensor_tensor(out=hT_lo[:, j, :], in0=ps[:, 4 + j % 4, :], scalar=gmix[:, j:j + 1],
                                               in1=hT_hi[:, j, :].bitcast(F32), op0=ALU.mult,
                                               op1=ALU.subtract).then_inc(hTlo_s, 1)

            def heads(ap):
                return ap.rearrange("p (h d) -> p h d", h=H)

            def rotate(q, b):
                gi, c = b // 8, b % NC
                cosv = mix[:, M_COS + c * DH:M_COS + (c + 1) * DH].unsqueeze(1)
                sinv = mix[:, M_SIN + c * DH:M_SIN + (c + 1) * DH].unsqueeze(1)
                wait_bank(v, gi, c)
                if q >= 2:
                    v.wait_ge(rot_tr, q - 1)
                src, dst, tmp = heads(ps[:, c, :]), heads(rot[:, q % 2, :]), heads(rtmp[:, :])
                hf = DH // 2
                nc.vector.tensor_tensor(dst, src, cosv.to_broadcast([P, H, DH]), ALU.mult)
                nc.vector.tensor_tensor(tmp[:, :, 0:hf], src[:, :, hf:DH], sinv[:, :, 0:hf].to_broadcast([P, H, hf]), ALU.mult)
                nc.vector.tensor_tensor(tmp[:, :, hf:DH], src[:, :, 0:hf], sinv[:, :, hf:DH].to_broadcast([P, H, hf]),
                                        ALU.mult).then_inc(drained_v, 1)
                v.wait_ge(drained_v, q + 1)
                nc.vector.tensor_tensor(dst, dst, tmp, ALU.add).then_inc(rot_s, 1)
                v.wait_ge(rot_s, q + 1)

            st_off = (0, 512, 896, 1152)
            st_bank = ((4, 0), (5, 0), (6, 0), (6, 256))

            def decayed(h):
                v.wait_ge(r_score, h + 1)
                v.wait_ge(*((dec01_in, 16) if h < 2 else (dec23_in, 16)))
                if h == 0:
                    v.wait_ge(a_tr, NC * H)
                if h == 1:
                    v.wait_ge(rot_tr, 16)
                if h >= 2:
                    v.wait_ge(r_pv, h - 1)
                st = (st0, st1)[h % 2]
                dec = decay01[:, h, :] if h < 2 else decay23[:, h - 2, :]
                for kc in range(NC):
                    bank, off = st_bank[kc]
                    w = S - kc * P
                    last = nc.vector.tensor_tensor(st[:, st_off[kc]:st_off[kc] + w], ps[:, bank, off:off + w],
                                                   dec[:, 0:w], ALU.mult)
                last.then_inc(r_st, 1)

            def head_stats(h):
                v.wait_ge(r_copy, h + 1)
                for c in range(NC):
                    last = nc.vector.bn_stats(stats6[:, h * NC + c, :], cat_ret[:, c, h * DH:(h + 1) * DH])
                link(last)
                for c in range(NC):
                    last = nc.vector.bn_aggr(mv[:, h * NC + c, :], stats6[:, h * NC + c, :])
                link(last)

            n_rot = 0
            v.wait_ge(mix_in, 16)
            for b in range(8 * NG):
                n, c = divmod(b, NC)
                gi, u = divmod(n, 2)
                if c == 0:
                    lo(n + 2)
                if RET + 1 <= b < RET + 1 + H:
                    decayed(b - RET - 1)
                if RET + 3 <= b < RET + 3 + H:
                    head_stats(b - RET - 3)
                if 21 <= b < 21 + NC * H:
                    j = b - 21
                    kw = (j % NC + 1) * P
                    v.wait_ge(a_exp, j + 1)
                    nc.vector.tensor_tensor_reduce(out=prob[:, j % 3, 0:kw], in0=prob[:, j % 3, 0:kw],
                                                   in1=mix[:, M_W + S - kw:M_W + S], scale=1.0, scalar=0.0, op0=ALU.mult,
                                                   op1=ALU.add, accum_out=small[:, 6, j:j + 1]).then_inc(a_prob, 1)
                    v.wait_ge(a_prob, j + 1)
                    nc.vector.reciprocal(small[:, 7, j:j + 1], small[:, 6, j:j + 1]).then_inc(a_rden, 1)
                if 20 <= b < 20 + NC * H:
                    j = b - 20
                    kw = (j % NC + 1) * P
                    v.wait_ge(a_score, j + 1)
                    if j >= 3:
                        v.wait_ge(a_tr, j - 2)
                    nc.vector.tensor_tensor_reduce(out=prob[:, j % 3, 0:kw], in0=ps[:, 4 + j % 2, 0:kw],
                                                   in1=mix[:, M_NEG + S - kw:M_NEG + S], scale=1.0, scalar=-3.0e38,
                                                   op0=ALU.add, op1=ALU.max,
                                                   accum_out=small[:, 4, j:j + 1]).then_inc(a_read, 1)
                    v.wait_ge(a_read, j + 1)
                    nc.vector.tensor_scalar(small[:, 5, j:j + 1], small[:, 4, j:j + 1], -SCALE, None, ALU.mult).then_inc(a_max, 1)
                if u == 1 and GROUPS[gi] in (AQ, AK, RQ, RK):
                    rotate(n_rot, b)
                    n_rot += 1
                if u == 1 and GROUPS[gi] == RG:
                    v.wait_ge(g_sig, c + 1)
                    nc.vector.tensor_tensor(rgt[:, c, :], rgt[:, c, :], probT[:, :], ALU.mult).then_inc(g_use, 1)
            head_stats(H - 1)
            for h in range(H):
                v.wait_ge(c_hi, h + 1)
                nc.vector.tensor_tensor(catT_lo[:, H + h, :], ps[:, 6 + h % 2, :], catT_hi[:, H + h, :].bitcast(F32),
                                        ALU.subtract).then_inc(c_lo, 1)

            nc.vector.tensor_copy(small[:, 14, :], mv[:, :, 0])
            nc.vector.tensor_scalar(small[:, 8, :], mv[:, :, 1], EPS, None, ALU.add).then_inc(gn_var, 1)
            v.wait_ge(gn_var, 1)
            v.wait_ge(gn_root, 1)
            inverse_root(small[:, 8, :], small[:, 9, :], small[:, 15, :], small[:, 13, :])
            v.wait_ge(g_use, NC)
            for h in range(H):
                for c in range(NC):
                    piece = cat_ret[:, c, h * DH:(h + 1) * DH]
                    last = nc.vector.tensor_scalar(piece, piece, small[:, 14, 4 * h + c:4 * h + c + 1],
                                                   small[:, 15, 4 * h + c:4 * h + c + 1], ALU.subtract, ALU.mult)
                link(last)
                piece = cat_ret[:, :, h * DH:(h + 1) * DH]
                nc.vector.tensor_tensor(piece, piece, rgt[:, :, h * DH:(h + 1) * DH], ALU.mult).then_inc(r_cat, 1)
            lo(16)
            for h in range(H):
                v.wait_ge(c_hi, H + h + 1)
                nc.vector.tensor_tensor(catT_lo[:, h, :], ps[:, 4 + h % 2, :], catT_hi[:, h, :].bitcast(F32),
                                        ALU.subtract).then_inc(c_lo, 1)
            lo(17)

            def residual(g):
                for c in range(NC):
                    wait_bank(v, NG + g, c)
                    piece = x1[:, c, g * UW:(g + 1) * UW]
                    nc.vector.tensor_tensor(piece, piece, ps[:, c, :], ALU.add).then_inc(x1_s, 1)

            residual(0)
            lo(18)
            lo(19)
            residual(1)

            v.wait_ge(sq, 2 * NC)
            nc.vector.tensor_scalar(small[:, 1, 0:NC], small[:, 0, 0:NC], 1.0 / D, EPS, ALU.mult, ALU.add).then_inc(var_s, 1)
            v.wait_ge(var_s, 2)
            v.wait_ge(root_s, 2)
            inverse_root(small[:, 1, 0:NC], small[:, 2, 0:NC], small[:, 3, 0:NC], small[:, 13, 0:NC])
            v.wait_ge(ffn_g_in, 16)
            v.wait_ge(x1_s, 2 * NC)
            for c in range(NC):
                nc.vector.scalar_tensor_tensor(out=hn[:, c, :], in0=x1[:, c, :], scalar=small[:, 3, c:c + 1],
                                               in1=g_row[:, :], op0=ALU.mult, op1=ALU.mult).then_inc(hn_s, 1)
            lo(20)
            v.wait_ge(logit_s, 1)
            link(nc.vector.tensor_copy(logits[:, :, :].rearrange("p c e -> p (c e)"), ps[:, 0, 0:NC * E]))
            for c in range(NC):
                last = nc.vector.max(out=top8[:, c, :], in_=logits[:, c, :])
            link(last)
            for c in range(NC):
                last = nc.vector.max_index(out=idx8[:, c, :], in_max=top8[:, c, :], in_values=logits[:, c, :])
            nc.vector.tensor_tensor(gates[:, :, :], top8[:, :, 0:TOPK], top8[:, :, 0:1].to_broadcast([P, NC, TOPK]),
                                    ALU.subtract).then_inc(top_s, 1)
            link(last)
            link(nc.vector.tensor_copy(idxf[:, :].rearrange("p (c k) -> p c k", c=NC), idx8[:, :, 0:TOPK]))
            link(nc.vector.tensor_tensor(onehot[:, :, :], cst[:, C_IOTA:C_IOTA + E].unsqueeze(1).to_broadcast([P, NC * TOPK, E]),
                                         idxf[:, :].unsqueeze(2).to_broadcast([P, NC * TOPK, E]), ALU.is_equal))
            nc.vector.tensor_reduce(out=masks[:, :, :], in_=onehot[:, :, :].rearrange("p (c k) e -> p c e k", c=NC),
                                    op=ALU.add, axis=AX.X).then_inc(mask_s, 1)
            v.wait_ge(gexp_s, 1)
            link(nc.vector.reduce_sum(small[:, 1, 0:NC], gates[:, :, :], axis=AX.X))
            link(nc.vector.reciprocal(small[:, 2, 0:NC], small[:, 1, 0:NC]))
            link(nc.vector.tensor_tensor(gates[:, :, :], gates[:, :, :],
                                         small[:, 2, 0:NC].unsqueeze(2).to_broadcast([P, NC, TOPK]), ALU.mult))
            nc.vector.tensor_copy(rows[:, :, 0], cst[:, C_TOK:C_TOK + NC * TOPK])
            nc.vector.tensor_copy(rows[:, :, 1], cst[:, C_DEST:C_DEST + NC * TOPK])
            nc.vector.tensor_copy(rows[:, :, 2].bitcast(F32), gates[:, :, :].rearrange("p c k -> p (c k)"))
            nc.vector.memset(rows[:, :, 3].bitcast(F32), 0.0)
            v.wait_ge(pos_s, 1)
            for c in range(NC):
                last = nc.vector.tensor_tensor(prod[:, c * TOPK:(c + 1) * TOPK, :],
                                               ps[:, 1, c * E:(c + 1) * E].unsqueeze(1).to_broadcast([P, TOPK, E]),
                                               onehot[:, c * TOPK:(c + 1) * TOPK, :], ALU.mult)
            link(last)
            link(nc.vector.reduce_sum(posk[:, :], prod[:, :, :], axis=AX.X))
            link(nc.vector.scalar_tensor_tensor(out=rowf[:, :], in0=posk[:, :], scalar=float(E), in1=idxf[:, :],
                                                op0=ALU.mult, op1=ALU.add))
            nc.vector.tensor_copy(row_idx[:, :], rowf[:, :]).then_inc(rows_s, 1)
            link(nc.vector.tensor_copy(counts[0:1, :], ps[0:1, 2, 0:E]))
            for k in range(3):
                last = nc.vector.tensor_scalar(ovf[0:1, k * E:(k + 1) * E], counts[0:1, :], float(P * (k + 1)), None, ALU.is_gt)
            link(last)
            link(nc.vector.tensor_tensor_scan(out=ovr[0:1, :], data0=cst[0:1, C_ONE:C_ONE + 3 * E], data1=ovf[0:1, :],
                                              initial=0.0, op0=ALU.mult, op1=ALU.add))
            nc.vector.tensor_copy(ov_total[0:1, 0:1], ovr[0:1, 3 * E - 1:3 * E])
            wide = [1, 16, 3 * E]
            link(nc.vector.tensor_tensor(ov_eq[0:1, :, :], ovr[0:1, :].unsqueeze(1).to_broadcast(wide),
                                         cst[0:1, C_NUM:C_NUM + 16].unsqueeze(2).to_broadcast(wide), ALU.is_equal))
            link(nc.vector.tensor_tensor(ov_eq[0:1, :, :], ov_eq[0:1, :, :], ovf[0:1, :].unsqueeze(1).to_broadcast(wide), ALU.mult))
            for k, col in ((0, C_OVE), (1, C_OVC)):
                for r in range(16):
                    last = nc.vector.tensor_tensor_reduce(out=ovt[0:1, :], in0=ov_eq[0:1, r, :], in1=cst[0:1, col:col + 3 * E],
                                                          scale=1.0, scalar=0.0, op0=ALU.mult, op1=ALU.add,
                                                          accum_out=ov_out[0:1, k, r:r + 1])
                    link(last)
            nc.vector.tensor_copy(ov_lists[0:1, :, :], ov_out[0:1, :, :]).then_inc(ov_s, 1)
            v.wait_ge(bias_in, 64)
            link(nc.vector.tensor_copy(bias[0:2 * E, :], bias_raw[0:2 * E, :]))
            nc.vector.tensor_tensor(bias[E:2 * E, :], bias_raw[E:2 * E, :], bias[E:2 * E, :].bitcast(F32),
                                    ALU.subtract).then_inc(bias_s, 1)

            def gate(hn0, units, i=0):
                half = hn0 % 2
                v.wait_ge(used, units)
                if hn0 > 0:
                    v.wait_ge(act_s, i * 2 + hn0)
                nc.vector.tensor_scalar(glu[:, :], ps[:, 2 * half, :], LIMIT, None, ALU.min).then_inc(glu_s, 1)
                nc.vector.tensor_scalar(lin[:, :], ps[:, 2 * half + 1, :], LIMIT, -LIMIT, ALU.min, ALU.max).then_inc(lin_s, 1)
                v.wait_ge(lin_s, i * 2 + (hn0 + 1))
                v.wait_ge(glu_s, i * 2 + (hn0 + 1))
                nc.vector.scalar_tensor_tensor(out=lin[:, :], in0=lin[:, :], scalar=1.0, in1=glu[:, :], op0=ALU.add,
                                               op1=ALU.mult).then_inc(gated_s, 1)

            def activated(hn0, i=0):
                half = hn0 % 2
                v.wait_ge(gated_s, i * 2 + (hn0 + 1))
                v.wait_ge(sig_s, i * 2 + (hn0 + 1))
                nc.vector.tensor_tensor(act[:, half * UW:(half + 1) * UW], lin[:, :], sig[:, :], ALU.mult).then_inc(act_s, 1)

            def tokens_lo(e, i=0):
                v.wait_ge(x_hi, i + (e + 1))
                nc.vector.tensor_tensor(xT_lo[:, :, :].rearrange("p k t -> p (k t)"),
                                        ps[:, 6:8, :].rearrange("p b t -> p (b t)"),
                                        xT_hi[:, :, :].rearrange("p k t -> p (k t)").bitcast(F32),
                                        ALU.subtract).then_inc(x_lo, 1)

            def features_lo(e, i=0):
                v.wait_ge(aT_hi, i + (e + 1))
                nc.vector.tensor_tensor(actT_lo[:, :, :].rearrange("p k t -> p (k t)"),
                                        ps[:, 6:8, :].rearrange("p b t -> p (b t)"),
                                        actT_hi[:, :, :].rearrange("p k t -> p (k t)").bitcast(F32),
                                        ALU.subtract).then_inc(aT_lo, 1)

            tokens_lo(0)
            for n in (21, 22, 23, 24):
                lo(n)
            gate(0, U_MOE + 4)
            lo(25)
            activated(0)
            for n in (26, 27, 28):
                lo(n)
            gate(1, U_MOE + 8)
            tokens_lo(1)
            activated(1)
            features_lo(0)
            with v.Fori(0, E - 1) as i:
                for n in (29, 30, 31, 32):
                    lo(n, i)
                gate(2, i * U_E + (U_LOOP + 4), i)
                lo(33, i)
                activated(2, i)
                for n in (34, 35, 36):
                    lo(n, i)
                gate(3, i * U_E + (U_LOOP + 8), i)
                tokens_lo(2, i)
                lo(37, i)
                activated(3, i)
                for n in (38, 39, 40):
                    lo(n, i)
                features_lo(1, i)
            lo(U_ALL - 1)

            v.wait_ge(act_s, 2 * E)
            v.wait_ge(ov_s, 1)
            total = v.value_load(ov_total[0:1, 0:1], min_val=0, max_val=NOVER)
            v.sem_inc(v_act, 1)
            with v.If(total > 0):
                with v.Fori(0, NOVER) as i:
                    with v.If(i < total):
                        v.wait_ge(v_tr, i * 2 + 1)
                        nc.vector.tensor_copy(xT32[:, :, :].rearrange("p k t -> p (k t)"),
                                              ps[:, 6:8, :].rearrange("p b t -> p (b t)")).then_inc(v_xT, 1)
                        for half in range(2):
                            v.wait_ge(v_act, i * 2 + (half + 1))
                            v.wait_ge(v_free, i * U_E + (RAW + 4 * (half + 1)))
                            nc.vector.tensor_scalar(glu[:, :], ps[:, 2 * half, :], LIMIT, None, ALU.min).then_inc(v_mid, 1)
                            nc.vector.tensor_scalar(lin[:, :], ps[:, 2 * half + 1, :], LIMIT, -LIMIT, ALU.min,
                                                    ALU.max).then_inc(v_chain, 1)
                            v.wait_ge(v_mid, i * 2 + (half + 1))
                            v.wait_ge(v_chain, i * 4 + (2 * half + 1))
                            nc.vector.scalar_tensor_tensor(out=lin[:, :], in0=lin[:, :], scalar=1.0, in1=glu[:, :],
                                                           op0=ALU.add, op1=ALU.mult).then_inc(v_chain, 1)
                            v.wait_ge(v_chain, i * 4 + (2 * half + 2))
                            v.wait_ge(v_sig, i * 2 + (half + 1))
                            nc.vector.tensor_tensor(act[:, half * UW:(half + 1) * UW], lin[:, :], sig[:, :],
                                                    ALU.mult).then_inc(v_act, 1)
                        v.wait_ge(v_tr, i * 2 + 2)
                        nc.vector.tensor_copy(actT32[:, :, :].rearrange("p k t -> p (k t)"),
                                              ps[:, 6:8, :].rearrange("p b t -> p (b t)")).then_inc(v_aT, 1)

            def final_sum(c):
                t = picked[c]
                v.wait_ge(picked_in[c], 16)
                link(nc.vector.tensor_tensor(t[:, 0:2, :], t[:, 0:2, :], t[:, 2:4, :], ALU.add))
                link(nc.vector.tensor_tensor(t[:, 0, :], t[:, 0, :], t[:, 1, :], ALU.add))
                nc.vector.tensor_tensor(x1[:, c, :], x1[:, c, :], t[:, 0, :], ALU.add).then_inc(f_sum, 1)

            def final_norm(c):
                v.wait_ge(f_sq, c + 1)
                nc.vector.tensor_scalar(small[:, 11, c:c + 1], small[:, 10, c:c + 1], 1.0 / D, EPS, ALU.mult,
                                        ALU.add).then_inc(f_var, 1)
                v.wait_ge(f_var, c + 1)
                v.wait_ge(f_root, c + 1)
                inverse_root(small[:, 11, c:c + 1], small[:, 12, c:c + 1], small[:, 3, c:c + 1], small[:, 13, c:c + 1])
                nc.vector.scalar_tensor_tensor(out=x1[:, c, :], in0=x1[:, c, :], scalar=small[:, 3, c:c + 1],
                                               in1=g_row[:, :], op0=ALU.mult, op1=ALU.mult).then_inc(f_out, 1)

            v.wait_ge(fin_g_in, 16)
            final_sum(0)
            for c in range(NC):
                if c + 1 < NC:
                    final_sum(c + 1)
                final_norm(c)

        @block.tensor
        def _(pe):
            mm = nc.tensor.matmul

            def three(out_ap, x_hi_ap, x_lo_ap, w_hi_ap, w_lo_ap, start, stop):
                mm(out_ap, x_hi_ap, w_hi_ap, start=start, stop=False)
                mm(out_ap, x_hi_ap, w_lo_ap, start=False, stop=False)
                return mm(out_ap, x_lo_ap, w_hi_ap, start=False, stop=stop)

            def unit_wait(n, i=0):
                pe.wait_ge(hi_done, i * U_E + (n + 1))
                pe.wait_ge(lo_done, i * U_E + (n + 1))

            def unit_part(n, k):
                return whi[:, n % SPLIT, k * UW:(k + 1) * UW], wlo[:, n % SPLIT, k * UW:(k + 1) * UW]

            pe.wait_ge(cst_in, 16)
            pe.wait_ge(xn_s, NC)
            for j in range(KD):
                if j >= 4:
                    pe.wait_ge(hTlo_s, j - 3)
                for c in range(NC):
                    last = nc.tensor.transpose(ps[:, 4 + j % 4, c * P:(c + 1) * P], xn[:, c, j * P:(j + 1) * P], ident)
                last.then_inc(xT_tr, 1)
            pe.wait_ge(hTlo_s, KD)

            drains = []
            for g in GROUPS:
                by_v = g in (AQ, AK, RQ, RK)
                drains.append((drained_v if by_v else drained_s, 4 * sum(s is (drained_v if by_v else drained_s) for s, _ in drains)))

            def project(b):
                n, c = divmod(b, NC)
                gi, u = divmod(n, 2)
                if c == 0:
                    unit_wait(n)
                if u == 0 and gi:
                    s, first = drains[gi - 1]
                    pe.wait_ge(s, first + c + 1)
                for k in range(KU):
                    kk = KU * u + k
                    w_hi_ap, w_lo_ap = unit_part(n, k)
                    last = three(ps[:, c, :], hT_hi[:, kk, c * P:(c + 1) * P], hT_lo[:, kk, c * P:(c + 1) * P],
                                 w_hi_ap, w_lo_ap, kk == 0, kk == KD - 1)
                finish(last, u == 1, c == NC - 1)

            def finish(last, bank_full, unit_done):
                if unit_done:
                    last.then_inc(used, 1)
                elif bank_full:
                    last.then_inc(proj, 1)

            def transpose_rot(q):
                pe.wait_ge(rot_s, q + 1)
                if q >= 2:
                    pe.wait_ge(rot_out, q - 1)
                if q == 8:
                    pe.wait_ge(a_read, NC * H)
                for h in range(H):
                    last = nc.tensor.transpose(ps[:, 4 + q % 2, h * P:(h + 1) * P], rot[:, q % 2, h * DH:(h + 1) * DH], ident)
                last.then_inc(rot_tr, 1)

            def scores(j):
                h, c = divmod(j, NC)
                if j == 0:
                    pe.wait_ge(rot_out, 8)
                if j >= 2:
                    pe.wait_ge(a_read, j - 1)
                mm(ps[:, 4 + j % 2, 0:(c + 1) * P], qT[:, h, c * P:(c + 1) * P], kT[:, h, 0:(c + 1) * P],
                   start=True, stop=True).then_inc(a_score, 1)

            def transpose_prob(j):
                pe.wait_ge(a_prob, j + 1)
                if j:
                    pe.wait_ge(a_pT, j)
                for kc in range(j % NC + 1):
                    last = nc.tensor.transpose(ps[:, 6, kc * P:(kc + 1) * P], prob[:, j % 3, kc * P:(kc + 1) * P], ident)
                last.then_inc(a_tr, 1)

            def values(j):
                h, c = divmod(j, NC)
                pe.wait_ge(a_pT, j + 1)
                if j == 0:
                    pe.wait_ge(drained_s, 4)
                if j:
                    pe.wait_ge(a_out, j)
                for kc in range(c + 1):
                    last = mm(ps[:, 7, 0:DH], probT[:, kc * P:(kc + 1) * P], avt[:, kc, h * DH:(h + 1) * DH],
                              start=(kc == 0), stop=(kc == c))
                last.then_inc(a_pv, 1)

            st_off = (0, 512, 896, 1152)
            st_bank = ((4, 0), (5, 0), (6, 0), (6, 256))

            def ret_scores(h):
                if h == 0:
                    pe.wait_ge(rot_out, 16)
                    pe.wait_ge(a_pT, NC * H)
                else:
                    pe.wait_ge(r_st, h)
                for kc in range(NC):
                    bank, off = st_bank[kc]
                    w = S - kc * P
                    last = mm(ps[:, bank, off:off + w], kT[:, h, kc * P:(kc + 1) * P], qT[:, h, kc * P:S], start=True, stop=True)
                last.then_inc(r_score, 1)

            def ret_values(h):
                pe.wait_ge(r_st, h + 1)
                if h == 0:
                    pe.wait_ge(drained_s, 2 * NC)
                    pe.wait_ge(a_out, NC * H)
                else:
                    pe.wait_ge(r_copy, h)
                st = (st0, st1)[h % 2]
                for qc in range(NC):
                    for kc in range(qc + 1):
                        o = st_off[kc] + (qc - kc) * P
                        last = mm(ps[:, 7, qc * P:(qc + 1) * P], st[:, o:o + P], rvt[:, kc, h * DH:(h + 1) * DH],
                                  start=(kc == 0), stop=(kc == qc))
                last.then_inc(r_pv, 1)

            n_rot = 0
            for b in range(8 * NG):
                project(b)
                step = b - 20
                if 3 <= step < NC * H + 3:
                    values(step - 3)
                if 2 <= step < NC * H + 2:
                    transpose_prob(step - 2)
                if 0 <= step < NC * H:
                    scores(step)
                rb = b - 2
                if rb >= 0 and (rb // NC) % 2 == 1 and GROUPS[rb // 8] in (AQ, AK, RQ, RK):
                    transpose_rot(n_rot)
                    n_rot += 1
                step = b - RET
                if 1 <= step < H + 1:
                    ret_values(step - 1)
                if 0 <= step < H:
                    ret_scores(step)

            def transpose_cat(q):
                src, bank = (cat_att, 6 + q % 2) if q < H else (cat_ret, 4 + q % 2)
                if q in (2, 3, 6, 7):
                    pe.wait_ge(c_lo, q - 1)
                if q == 0:
                    pe.wait_ge(a_out, NC * H)
                    pe.wait_ge(r_st, H)
                if q == 1:
                    pe.wait_ge(r_copy, H)
                if q >= H:
                    pe.wait_ge(r_cat, q - H + 1)
                h = q % H
                for c in range(NC):
                    last = nc.tensor.transpose(ps[:, bank, c * P:(c + 1) * P], src[:, c, h * DH:(h + 1) * DH], ident)
                last.then_inc(c_tr, 1)

            for q in range(H):
                transpose_cat(q)

            def out_project(n, c):
                g, part = divmod(n - U_OUT, 2)
                if c == 0:
                    unit_wait(n)
                if part == 0 and g == 0:
                    pe.wait_ge(drained_s, 2 * NC + c + 1)
                if part == 0 and g == 1:
                    pe.wait_ge(x1_s, c + 1)
                if c == 0:
                    pe.wait_ge(c_lo, H if (part == 0) else 2 * H)
                for k in range(KU):
                    kk = KU * (1 - part) + k
                    w_hi_ap, w_lo_ap = unit_part(n, k)
                    last = three(ps[:, c, :], catT_hi[:, kk, c * P:(c + 1) * P], catT_lo[:, kk, c * P:(c + 1) * P],
                                 w_hi_ap, w_lo_ap, part == 0 and k == 0, part == 1 and k == KU - 1)
                finish(last, part == 1, c == NC - 1)

            for c in range(NC):
                out_project(U_OUT, c)
            for q in range(H, 2 * H):
                transpose_cat(q)
            for n in range(U_OUT + 1, U_MOE):
                for c in range(NC):
                    out_project(n, c)

            for j in range(KD):
                if j == 0:
                    pe.wait_ge(hn_s, NC)
                if j < 4:
                    pe.wait_ge(r_copy, H)
                else:
                    pe.wait_ge(hnT_s, j - 3)
                for c in range(NC):
                    last = nc.tensor.transpose(ps[:, 4 + j % 4, c * P:(c + 1) * P], hn[:, c, j * P:(j + 1) * P], ident)
                last.then_inc(hn_tr, 1)
            pe.wait_ge(hnT_s, KD)
            pe.wait_ge(router_in, 32)
            pe.wait_ge(x1_s, 2 * NC)
            for c in range(NC):
                o = ps[:, 0, c * E:(c + 1) * E]
                mm(o, ones, br[:, :], start=True, stop=False)
                for j in range(KD):
                    last = mm(o, hnT[:, j, c * P:(c + 1) * P], wr[:, j, :], start=False, stop=(j == KD - 1))
            last.then_inc(logit_s, 1)
            pe.wait_ge(mask_s, 1)
            tri = cst[:, C_TRI:C_TRI + P]
            for c in range(NC):
                o = ps[:, 1, c * E:(c + 1) * E]
                for cc in range(c):
                    mm(o, ones, masks[:, cc, :], start=(cc == 0), stop=False)
                mm(o, tri, masks[:, c, :], start=(c == 0), stop=True)
            for c in range(NC):
                last = mm(ps[:, 2, 0:E], ones, masks[:, c, :], start=(c == 0), stop=(c == NC - 1))
            last.then_inc(pos_s, 1)

            def tokens(e, i=0):
                pe.wait_ge(gathered, i * 16 + 16 * (e + 1))
                if e > 1:
                    pe.wait_ge(aT_hi, i + (e - 1))
                    pe.wait_ge(aT_lo, i + (e - 1))
                for j in range(KD):
                    last = nc.tensor.transpose(ps[:, 6 + j // 4, (j % 4) * P:(j % 4 + 1) * P], xg[:, j * P:(j + 1) * P], ident)
                last.then_inc(x_tr, 1)

            def features(e, i=0):
                pe.wait_ge(act_s, i * 2 + 2 * (e + 1))
                pe.wait_ge(x_hi, i + (e + 2))
                pe.wait_ge(x_lo, i + (e + 2))
                for j in range(KD):
                    last = nc.tensor.transpose(ps[:, 6 + j // 4, (j % 4) * P:(j % 4 + 1) * P], act[:, j * P:(j + 1) * P], ident)
                last.then_inc(act_tr, 1)

            def half_matrix(n0, i, bank, sel, b0, x_hi_t, x_lo_t):
                mm(ps[:, bank, :], sel[:, :], bias[:, b0:b0 + UW], start=True, stop=False)
                for u in range(2):
                    unit_wait(n0 + u, i)
                    for k in range(KU):
                        kk = KU * u + k
                        w_hi_ap, w_lo_ap = unit_part(n0 + u, k)
                        last = three(ps[:, bank, :], x_hi_t[:, kk, :], x_lo_t[:, kk, :], w_hi_ap, w_lo_ap, False, kk == KD - 1)
                    last.then_inc(used, 1)

            def gate_up(n0, e, i=0):
                pe.wait_ge(sel_gu_s, i + (e + 1))
                pe.wait_ge(x_hi, i + (e + 1))
                pe.wait_ge(x_lo, i + (e + 1))
                for q in range(4):
                    if e > 0 and q % 2 == 0:
                        pe.wait_ge(lin_s, i * 2 + (2 * e + q // 2 - 1))
                    half_matrix(n0 + 2 * q, i, q, sel_gu, GU_COLS[q] * UW, xT_hi, xT_lo)

            def down(n0, e, i=0):
                pe.wait_ge(sel_dn_s, i + (e + 1))
                pe.wait_ge(aT_hi, i + (e + 1))
                pe.wait_ge(aT_lo, i + (e + 1))
                pe.wait_ge(y_s, i + (e + 1))
                for q in range(2):
                    half_matrix(n0 + 2 * q, i, 4 + q, sel_dn, 2 * D + q * UW, actT_hi, actT_lo)

            pe.wait_ge(bias_s, 1)
            pe.wait_ge(ov_s, 1)
            tokens(0)
            gate_up(U_MOE, 0)
            pe.wait_ge(x_lo, 1)
            tokens(1)
            with pe.Fori(0, E - 1) as i:
                features(0, i)
                gate_up(U_LOOP, 1, i)
                tokens(2, i)
                down(U_LOOP + U_GU, 0, i)
            features(E - 1)
            down(U_ALL - U_DN, E - 1)

            for r in range(RAW):
                pe.sem_inc(v_free, 1)
            pe.wait_ge(ov_s, 1)
            total = pe.value_load(ov_total[0:1, 0:1], min_val=0, max_val=NOVER)
            with pe.If(total > 0):
                with pe.Fori(0, NOVER) as i:
                    with pe.If(i < total):
                        def whole_matrix(q, bank, b0, x_t):
                            mm(ps[:, bank, :], sel_gu[:, :], bias[:, b0:b0 + UW], start=True, stop=False)
                            for u in range(2 * q, 2 * q + 2):
                                pe.wait_ge(v_full[u % RAW], i * (16 * U_E // RAW) + 16 * (u // RAW + 1))
                                for k in range(KU):
                                    kk = KU * (u % 2) + k
                                    last = mm(ps[:, bank, :], x_t[:, kk, :], raw[:, u % RAW, k * UW:(k + 1) * UW],
                                              start=False, stop=(kk == KD - 1))
                                last.then_inc(v_free, 1)

                        pe.wait_ge(v_gather, i * 16 + 16)
                        pe.wait_ge(v_sel, i + 1)
                        for j in range(KD):
                            last = nc.tensor.transpose(ps[:, 6 + j // 4, (j % 4) * P:(j % 4 + 1) * P], xg[:, j * P:(j + 1) * P], ident)
                        last.then_inc(v_tr, 1)
                        pe.wait_ge(v_xT, i + 1)
                        for q in range(4):
                            whole_matrix(q, q, GU_COLS[q] * UW, xT32)
                        pe.wait_ge(v_act, i * 2 + 3)
                        for j in range(KD):
                            last = nc.tensor.transpose(ps[:, 6 + j // 4, (j % 4) * P:(j % 4 + 1) * P], act[:, j * P:(j + 1) * P], ident)
                        last.then_inc(v_tr, 1)
                        pe.wait_ge(v_aT, i + 1)
                        for q in (4, 5):
                            whole_matrix(q, q, 2 * D + (q - 4) * UW, actT32)


_INS = ["x", "norm_mix_g", "w_in", "w_out", "norm_ffn_g", "w_router", "b_router",
        "w_gate_up", "b_gate_up", "w_down", "b_down", "norm_final_g"]


def kernel(**inputs):
    import numpy as _np
    import concourse.bacc as _bacc
    from concourse import mybir as _mybir
    from concourse.bass_utils import run_bass_kernel_spmd as _run

    nc = _bacc.Bacc("TRN2", target_bir_lowering=False, num_devices=1)
    arrays, args = {}, []
    for name in _INS:
        a = _np.ascontiguousarray(inputs[name])
        arrays[f"in_{name}"] = a
        args.append(nc.dram_tensor(f"in_{name}", a.shape, _mybir.dt.from_np(a.dtype), kind="ExternalInput").ap())
    out = nc.dram_tensor("out", (1, S, D), F32, kind="ExternalOutput").ap()
    build(nc, *args, out)
    r = _run(nc, [arrays], core_ids=[0])
    return r.results[0]["out"]
```

```python
import concourse.bass as bass
from concourse import mybir
import numpy as np

F32 = mybir.dt.float32
F32R = mybir.dt.float32r
U32 = mybir.dt.uint32
I32 = mybir.dt.int32
ALU = mybir.AluOpType
ACT = mybir.ActivationFunctionType
AX = mybir.AxisListType

P = 128
S = 512
D = 1024
NC = S // P
KD = D // P
H = 4
DH = 128
GW = H * DH
E = 32
TOPK = 4
EPS = 1e-5
LIMIT = 7.0
ALPHA = 1.702
SCALE = float(DH) ** -0.5
BIG_NEG = -1.0e30

KU = 4
UW = 512
UNIT = KU * UW
RAW = 4
RAW_E = 6
SPLIT = 3
RQ, RK, RV, RG, AQ, AK, AV = range(7)
GROUPS = [AQ, AK, AV, RV, RQ, RK, RG]
NG = len(GROUPS)
RET = 8 * NG - 6
U_OUT = 2 * NG
U_MOE = U_OUT + 4
U_GU = 8
U_DN = 4
U_E = U_GU + U_DN
U_LOOP = U_MOE + U_GU
U_ALL = U_MOE + E * U_E
NOVER = 15

C_ID = 0
C_TRI = C_ID + P
C_ONE = C_TRI + P
C_IOTA = C_ONE + P
C_TOK = C_IOTA + E
C_DEST = C_TOK + NC
C_OFF = C_DEST + NC
C_SEL = C_OFF + 4
C_OVE = C_SEL + 40
C_OVC = C_OVE + 3 * E
C_NUM = C_OVC + 3 * E
C_SMALL = C_NUM + 16
M_COS = 0
M_SIN = M_COS + NC * DH
M_W = M_SIN + NC * DH
M_NEG = M_W + S
M_SMALL = M_NEG + S


def slot_of(n):
    return n % RAW if n < U_MOE else (n - U_MOE + 2) % RAW_E


def last_in_slot(n):
    return next((m for m in range(n - 1, -1, -1) if slot_of(m) == slot_of(n)), None)


def constants():
    small = np.zeros((P, C_SMALL), np.float32)
    p = np.arange(P)
    small[:, C_ID:C_ID + P] = np.eye(P)
    small[:, C_TRI:C_TRI + P] = (p[:, None] < p[None, :])
    small[:, C_ONE:C_ONE + P] = 1.0
    small[:, C_IOTA:C_IOTA + E] = np.arange(E)[None]
    token = np.arange(NC)[None] * P + p[:, None]
    small[:, C_TOK:C_TOK + NC] = token - S
    small[:, C_DEST:C_DEST + NC] = (token - S) * TOPK
    small[:, C_OFF:C_OFF + 4] = np.array([S, S * TOPK, 0, 0])[None]
    for e in range(E):
        small[e, C_SEL + e] = 1.0
        small[E + e, C_SEL + e] = 1.0
    pair = np.arange(3 * E)
    small[:, C_OVE:C_OVE + 3 * E] = (pair % E)[None]
    small[:, C_OVC:C_OVC + 3 * E] = ((pair // E + 1) * P)[None]
    small[:, C_NUM:C_NUM + 16] = np.arange(1, 17)[None]

    mix = np.zeros((P, M_SMALL), np.float32)
    inv = np.float32(10000.0) ** (-np.arange(0, DH, 2, dtype=np.float32) / np.float32(DH))
    ang = np.arange(S, dtype=np.float32)[:, None] * inv[None, :]
    cos, sin = np.cos(ang), np.sin(ang)
    cc = np.concatenate([cos, cos], 1).reshape(NC, P, DH).transpose(1, 0, 2)
    ss = np.concatenate([-sin, sin], 1).reshape(NC, P, DH).transpose(1, 0, 2)
    mix[:, M_COS:M_COS + NC * DH] = cc.reshape(P, -1)
    mix[:, M_SIN:M_SIN + NC * DH] = ss.reshape(P, -1)
    dist = (NC - 1) * P + p[:, None] - np.arange(S)[None, :]
    w = np.zeros((P, S), np.float32)
    for window, dil in ((128, 1), (512, 4), (2048, 16)):
        w += (dist >= 0) & (dist % dil == 0) & (dist // dil <= window // dil)
    mix[:, M_W:M_W + S] = w
    mix[:, M_NEG:M_NEG + S] = np.where(w > 0, 0.0, BIG_NEG)

    m = np.arange(S)[None, :] - p[:, None]
    log_g = np.log1p(-(2.0 ** (-5.0 - np.arange(H, dtype=np.float64))))
    dec = np.where(m[None] >= 0, np.exp(np.maximum(m, 0)[None] * log_g[:, None, None]), 0.0) * DH ** -0.5
    decay = dec.transpose(1, 0, 2).reshape(P, H * S).astype(np.float32)
    slots = np.broadcast_to(np.arange(S, dtype=np.float32)[None], (P, S)).copy()
    return small, mix, decay, slots


def build(nc, x, norm_mix_g, w_in, w_out, norm_ffn_g, w_router, b_router,
          w_gate_up, b_gate_up, w_down, b_down, norm_final_g, out):
    small_np, mix_np, decay_np, slots_np = constants()
    small_d = nc.inline_tensor(small_np, name="const_small").ap()
    mix_d = nc.inline_tensor(mix_np, name="const_mix").ap()
    decay_d = nc.inline_tensor(decay_np, name="const_decay").ap()
    slots_d = nc.inline_tensor(slots_np, name="const_slots").ap()
    h_rows = nc.dram_tensor("h_rows", [S, D], F32).ap()
    y_rows = nc.dram_tensor("y_rows", [S * TOPK, D], F32).ap()

    def place(offset, name, cols, dt=F32):
        t = nc.alloc_sbuf_tensor_at(name, [P, *cols], dt, offset=offset)
        return t, (offset + int(np.prod(cols)) * 4 + 31) // 32 * 32

    base = (nc.sbuf_base + 63) // 64 * 64
    raw, o = place(base, "raw", [RAW, UNIT])
    whi, o = place(o, "whi", [SPLIT, UNIT], F32R)
    wlo, o = place(o, "wlo", [SPLIT, UNIT], F32R)
    x1, o = place(o, "x1", [NC, D])
    cst, o = place(o, "cst", [C_SMALL])
    gmix, o = place(o, "gmix", [KD])
    row_rms, o = place(o, "row_rms", [NC])
    small, o = place(o, "small", [16, 16])
    mv, o = place(o, "mv", [NC * H, 2])
    stats6, o = place(o, "stats6", [NC * H, 6])
    ov_lists, o = place(o, "ov_lists", [2, 16], I32)
    ov_total, o = place(o, "ov_total", [2], I32)
    idx_gather, o = place(o, "idx_gather", [1], U32)
    idx_scatter, o = place(o, "idx_scatter", [1], U32)
    area = (o + 63) // 64 * 64
    K = 1024
    hT_hi, _ = place(area, "hT_hi", [KD, S], F32R)
    hT_lo, _ = place(area + 16 * K, "hT_lo", [KD, S], F32R)
    qT, _ = place(area + 32 * K, "qT", [H, S])
    kT, _ = place(area + 40 * K, "kT", [H, S])
    avt, _ = place(area + 48 * K, "avt", [NC, GW])
    rvt, _ = place(area + 56 * K, "rvt", [NC, GW])
    rgt, _ = place(area + 64 * K, "rgt", [NC, GW])
    cat_att, _ = place(area + 72 * K, "cat_att", [NC, GW])
    rot, _ = place(area + 80 * K, "rot", [2, GW])
    rtmp, _ = place(area + 84 * K, "rtmp", [GW])
    prob, _ = place(area + 86 * K, "prob", [3, S])
    probT, _ = place(area + 92 * K, "probT", [S])
    mix, o = place(area + 94 * K, "mix", [M_SMALL])
    assert o <= nc.sbuf_usable_end, (o, nc.sbuf_usable_end)
    raw_a, _ = place(area + 80 * K, "raw_a", [UNIT])
    raw_b, _ = place(area + 94 * K, "raw_b", [UNIT])
    squares0, _ = place(area + 32 * K, "squares0", [NC, D])
    catT_hi, _ = place(area, "catT_hi", [KD, S], F32R)
    catT_lo, _ = place(area + 16 * K, "catT_lo", [KD, S], F32R)
    cat_ret, _ = place(area + 48 * K, "cat_ret", [NC, GW])
    st0, _ = place(area + 86 * K, "st0", [1280])
    st1, _ = place(area + 80 * K, "st1", [1280])
    decay23, _ = place(area + 94 * K, "decay23", [2, S])
    decay01, _ = place(area + 98 * K, "decay01", [2, S])
    rT, _ = place(area + 48 * K, "rT", [KD, S])
    hn, _ = place(area + 32 * K, "hn", [NC, D])
    g_row, _ = place(area + 64 * K, "g_row", [D])
    wr, o = place(area + 72 * K, "wr", [KD, E])
    gffn, o = place(o, "gffn", [KD])
    br, o = place(o, "br", [E])
    logits, o = place(o, "logits", [NC, E])
    onehot, o = place(o, "onehot", [NC * TOPK, E])
    masks, o = place(o, "masks", [NC, E], F32R)
    tri_r, o = place(o, "tri_r", [P], F32R)
    ones_r, o = place(o, "ones_r", [P], F32R)
    pair_gate, o = place(o, "pair_gate", [NC, E])
    pair_rank, o = place(o, "pair_rank", [NC, E])
    pair_pos, o = place(o, "pair_pos", [NC, E])
    prod, _ = place(area + 70 * K, "prod", [NC * TOPK, E])
    top8, o = place(o, "top8", [NC, 8])
    idx8, o = place(o, "idx8", [NC, 8], U32)
    idxf, o = place(o, "idxf", [NC * TOPK])
    gates, o = place(o, "gates", [NC, TOPK])
    assert o <= area + 80 * K
    counts, o = place(area + 68 * K, "counts", [E])
    ovf, o = place(o, "ovf", [3 * E])
    ovr, o = place(o, "ovr", [3 * E])
    ov_out, o = place(o, "ov_out", [2, 16])
    assert o <= area + 70 * K
    squares, _ = place(area + 88 * K, "squares", [D])
    ov_eq, o = place(area, "ov_eq", [16, 3 * E])
    ovt, o = place(o, "ovt", [16, 3 * E])
    slots, o = place(o, "slots", [S])
    has, o = place(o, "has", [NC, P], F32R)
    pairs, o = place(o, "pairs", [NC, E + 2, 8])
    pair, o = place(o, "pair", [NC, 8], F32R)
    tab, o = place(o, "tab", [E + 1, 4])
    tab_over, o = place(o, "tab_over", [4])
    slot_sums, o = place(o, "slot_sums", [4])
    slot_row, o = place(o, "slot_row", [P])
    assert o <= area + 24 * K
    xT_hi, _ = place(area + 24 * K, "xT_hi", [KD, P], F32R)
    xT_lo, _ = place(area + 28 * K, "xT_lo", [KD, P], F32R)
    bias_raw, _ = place(area + 52 * K, "bias_raw", [3 * D])
    xg, _ = place(area + 48 * K, "xg", [D])
    act, _ = place(area + 52 * K, "act", [D])
    actT_hi, _ = place(area + 56 * K, "actT_hi", [KD, P], F32R)
    actT_lo, _ = place(area + 60 * K, "actT_lo", [KD, P], F32R)
    y, _ = place(area + 72 * K, "y", [D])
    glu, o = place(area + 76 * K, "glu", [UW])
    lin, o = place(o, "lin", [UW])
    bias, _ = place(area + 32 * K, "bias", [3 * D], F32R)
    sig, _ = place(area + 92 * K, "sig", [UW])
    sel_gu, o = place(area + 44 * K, "sel_gu", [P], F32R)
    sel_dn, o = place(o, "sel_dn", [P], F32R)
    xT32, _ = place(area + 24 * K, "xT32", [KD, P])
    actT32, _ = place(area + 56 * K, "actT32", [KD, P])
    picked = [place(at, f"picked{c}", [TOPK, D])[0] for c, at in enumerate((area, area + 32 * K, base, base + 16 * K))]

    ps = nc.alloc_psum_tensor("ps", [P, 8, UW], F32)

    ident = cst[:, C_ID:C_ID + P]
    ones = cst[:, C_ONE:C_ONE + P]

    def sem(name):
        return nc.alloc_semaphore(name)

    raw_full = [sem(f"raw_full{r}") for r in range(RAW)]
    moe_full = [sem(f"moe_full{r}") for r in range(RAW_E)]
    hi_done, lo_done = sem("hi_done"), sem("lo_done")
    used = sem("units_used")
    x_in = [sem(f"x_in{c}") for c in range(NC)]
    cst_in, mix_in, gmix_in = sem("cst_in"), sem("mix_in"), sem("gmix_in")
    slots_in, pairs_init, ones_s = sem("slots_in"), sem("pairs_cleared"), sem("ones_ready")
    pairs_s, has_s, pair_tr, tab_raw, tab_s = (sem("pairs_ready"), sem("slots_of_expert"), sem("table_product"),
                                               sem("table_read"), sem("table_ready"))
    counts_s, bias_hi, total_s = sem("counts_ready"), sem("bias_hi_ready"), sem("total_ready")
    sq, var_s, root_s, rstd_s = sem("squares"), sem("variance"), sem("root"), sem("rstd")
    xT_tr = sem("x_transposed")
    hThi_s, hTlo_s = sem("hT_hi_ready"), sem("hT_lo_ready")
    dve = sem("vector_chain")
    proj = sem("projected")
    drained_v, drained_s = sem("drained_by_vector"), sem("drained_by_scalar")
    rot_s, rot_tr, rot_out = sem("rotated"), sem("rot_transposed"), sem("rot_stored")
    a_score, a_max, a_exp, a_prob = sem("att_scores"), sem("att_max"), sem("att_exp"), sem("att_prob")
    a_tr, a_pT, a_pv, a_out = sem("att_transposed"), sem("att_probT"), sem("att_pv"), sem("att_out")
    dec01_in, dec23_in = sem("decay01_in"), sem("decay23_in")
    r_score, r_st, r_pv, r_copy = sem("ret_scores"), sem("ret_decayed"), sem("ret_pv"), sem("ret_copied")
    g_sig, g_use, r_cat = sem("gate_sigmoid"), sem("gate_used"), sem("ret_ready")
    gn_var, gn_root = sem("group_variance"), sem("group_root")
    c_tr, c_hi, c_lo = sem("cat_transposed"), sem("cat_hi"), sem("cat_lo")
    x1_s = sem("residual_added")
    ffn_g_in, router_in = sem("ffn_gain_in"), sem("router_in")
    hn_s, hn_out, hn_gain = sem("hn_ready"), sem("hn_stored"), sem("hn_times_gain")
    r_tr, rT_s, wr_s = sem("residual_transposed"), sem("rT_ready"), sem("router_weights_ready")
    logit_s, mask_s, pos_s = sem("logits_ready"), sem("masks_ready"), sem("positions_ready")
    top_s, gexp_s = sem("top_ready"), sem("gate_exp")
    a_read, a_rden = sem("att_scores_read"), sem("att_row_sums")
    v_chain = sem("over_vector_chain")
    bias_in, bias_s, ov_s = sem("bias_in"), sem("bias_ready"), sem("overflow_listed")
    pool = sem("pool_chain")
    sel_gu_s, sel_dn_s = sem("select_gate_up"), sem("select_down")
    gathered, scattered = sem("gathered"), sem("scattered")
    x_tr, x_hi, x_lo = sem("tokens_transposed"), sem("tokens_hi"), sem("tokens_lo")
    glu_s, lin_s, gated_s, sig_s, act_s = (sem("glu_clamped"), sem("lin_clamped"), sem("gated"),
                                           sem("sigmoid_ready"), sem("act_ready"))
    act_tr, aT_hi, aT_lo = sem("act_transposed"), sem("actT_hi"), sem("actT_lo")
    y_s, y_free = sem("y_ready"), sem("y_free")
    fin_g_in, rows_done = sem("final_gain_in"), sem("all_rows_stored")
    picked_in = [sem(f"picked_in{h}") for h in range(2 * NC)]
    f_pair, f_gain = sem("final_pair_sum"), sem("final_times_gain")
    f_sum, f_sq, f_var, f_root, f_out, stored = (sem("final_sum"), sem("final_squares"), sem("final_variance"),
                                         sem("final_root"), sem("final_rows"), sem("outputs_stored"))
    v_full = [sem(f"over_raw_full{r}") for r in range(RAW)]
    v_has, v_table, v_raw, v_tab, v_free, v_sel, v_gather, v_tr, v_xT, v_sig, v_act, v_aT, v_y, v_scatter, v_mid = (
        sem("over_slots"), sem("over_table_product"), sem("over_table_read"), sem("over_table"),
        sem("over_raw_free"), sem("over_select"), sem("over_gathered"), sem("over_transposed"),
        sem("over_tokens"), sem("over_sigmoid"), sem("over_act"), sem("over_actT"),
        sem("over_y"), sem("over_scattered"), sem("over_glu"))

    win_v = w_in[0].rearrange("(k p) (g c) -> p g k c", p=P, c=UW)
    wout_v = w_out[0].rearrange("(k p) (g c) -> p g k c", p=P, c=UW)
    wgu_v = w_gate_up[0].rearrange("e (k p) (g c) -> p e g k c", p=P, c=UW)
    wdn_v = w_down[0].rearrange("e (k p) (g c) -> p e g k c", p=P, c=UW)

    def mixer_source(n):
        if n < U_OUT:
            return win_v[:, GROUPS[n // 2], KU * (n % 2):KU * (n % 2) + KU, :]
        g, part = divmod(n - U_OUT, 2)
        return wout_v[:, g, KU * (1 - part):KU * (1 - part) + KU, :]

    GU_COLS = [0, 2, 1, 3]

    def raw_slot(r):
        return raw[:, r, :] if r < RAW else (raw_a, raw_b)[r - RAW][:, :]

    def raw4(r):
        return raw_slot(r).rearrange("p (k c) -> p k c", k=KU)

    def full(n, i=0):
        if n < U_MOE:
            return raw_full[slot_of(n)], 16 * (n // RAW + 1)
        return moe_full[slot_of(n)], i * (16 * U_E // RAW_E) + 16 * ((n - U_MOE) // RAW_E + 1)

    def wait_bank(eng, g, c):
        if c < NC - 1:
            eng.wait_ge(proj, (NC - 1) * g + c + 1)
        else:
            eng.wait_ge(used, 2 * g + 2)

    block = nc.Block()
    with block as block:
        @block.sync
        def _(sp):
            def load(n, i, source):
                if last_in_slot(n) is not None:
                    sp.wait_ge(lo_done, i * U_E + (last_in_slot(n) + 1))
                elif n >= U_MOE:
                    sp.wait_ge(r_pv, H)
                    sp.wait_ge(rot_tr, 16)
                sp.dma_start(raw4(slot_of(n)), source).then_inc(full(n)[0], 16)

            load(0, 0, mixer_source(0))
            for c in range(NC):
                sp.dma_start(x1[:, c, :], x[0, c * P:(c + 1) * P, :]).then_inc(x_in[c], 16)
            for n in range(1, U_LOOP):
                if n == U_MOE + RAW_E:
                    for c in range(NC):
                        sp.wait_ge(hn_s, c + 1)
                        sp.dma_start(h_rows[c * P:(c + 1) * P, :], hn[:, c, :]).then_inc(hn_out, 16)
                if n < U_MOE:
                    load(n, 0, mixer_source(n))
                else:
                    u = n - U_MOE
                    load(n, 0, wgu_v[:, 0, GU_COLS[u // 2], KU * (u % 2):KU * (u % 2) + KU, :])
            with sp.Fori(0, E - 1) as i:
                for u in range(U_E):
                    k0 = KU * (u % 2)
                    if u < U_GU:
                        src = wgu_v[:, bass.ds(i + 1, 1), GU_COLS[u // 2], k0:k0 + KU, :]
                    else:
                        src = wdn_v[:, bass.ds(i, 1), (u - U_GU) // 2, k0:k0 + KU, :]
                    load(U_LOOP + u, i, src.rearrange("p e k c -> p (e k) c"))
            for u in range(U_DN):
                load(U_ALL - U_DN + u, 0, wdn_v[:, E - 1, u // 2, KU * (u % 2):KU * (u % 2) + KU, :])

            sp.wait_ge(ov_s, 1)
            sp.wait_ge(lo_done, U_ALL)
            total = sp.value_load(ov_total[0:1, 0:1], min_val=0, max_val=NOVER)
            with sp.If(total > 0):
                with sp.Fori(0, NOVER) as i:
                    with sp.If(i < total):
                        e = sp.value_load(ov_lists[0:1, 0, bass.ds(i, 1)], min_val=0, max_val=E - 1)
                        for u in range(U_E):
                            k0 = KU * (u % 2)
                            sp.wait_ge(v_free, i * U_E + (u + 1))
                            if u < U_GU:
                                src = wgu_v[:, bass.ds(e, 1), GU_COLS[u // 2], k0:k0 + KU, :]
                            else:
                                src = wdn_v[:, bass.ds(e, 1), (u - U_GU) // 2, k0:k0 + KU, :]
                            sp.dma_start(raw4(u % RAW), src.rearrange("p e k c -> p (e k) c")).then_inc(v_full[u % RAW], 16)

            sp.wait_ge(rows_done, 1)
            y_view = y_rows.rearrange("(c p k) d -> c p k d", p=P, k=TOPK)
            for c in range(NC):
                for k in range(0, TOPK, 2):
                    sp.dma_start(picked[c][:, k:k + 2, :], y_view[c][:, k:k + 2, :]).then_inc(picked_in[2 * c + k // 2], 16)
            for c in range(NC):
                sp.wait_ge(f_out, c + 1)
                sp.dma_start(out[0, c * P:(c + 1) * P, :], picked[c][:, 0, :]).then_inc(stored, 16)
            sp.wait_ge(stored, 16 * NC)

        @block.gpsimd
        def _(pl):
            chain = [0]

            def link(ins):
                chain[0] += 1
                ins.then_inc(pool, 1)
                pl.wait_ge(pool, chain[0])

            pl.wait_ge(a_prob, NC * H)
            pl.dma_start(decay01[:, :, :], decay_d[:, 0:2 * S].rearrange("p (h m) -> p h m", h=2)).then_inc(dec01_in, 16)
            pl.wait_ge(rot_s, 16)
            pl.dma_start(decay23[:, :, :], decay_d[:, 2 * S:4 * S].rearrange("p (h m) -> p h m", h=2)).then_inc(dec23_in, 16)
            pl.wait_ge(c_tr, H)
            with nc.allow_non_contiguous_dma(reason="rows of 128 bytes, and 1024 gains onto partitions"):
                pl.dma_start(wr[:, :, :], w_router[0].rearrange("(k p) e -> p k e", p=P)).then_inc(router_in, 16)
                pl.dma_start(gffn[:, :], norm_ffn_g[0].rearrange("(k p) -> p k", p=P)).then_inc(router_in, 16)
                pl.dma_start(br[:, :], b_router[0:1, :].to_broadcast([P, E])).then_inc(router_in, 16)
            pl.wait_ge(r_cat, H)
            pl.dma_start(g_row[:, :], norm_ffn_g[0:1, :].to_broadcast([P, D])).then_inc(ffn_g_in, 16)
            pl.wait_ge(ffn_g_in, 16)
            pl.wait_ge(cst_in, 16)
            nc.gpsimd.tensor_copy(tri_r[:, :], cst[:, C_TRI:C_TRI + P]).then_inc(ones_s, 1)
            nc.gpsimd.tensor_copy(ones_r[:, :], ones).then_inc(ones_s, 1)
            for c in range(NC):
                pl.wait_ge(x1_s, NC + c + 1)
                nc.gpsimd.tensor_tensor(hn[:, c, :], x1[:, c, :], g_row[:, :], ALU.mult).then_inc(hn_gain, 1)
            pl.wait_ge(logit_s, 2)
            pl.dma_start(slots[:, :], slots_d).then_inc(slots_in, 16)
            link(nc.gpsimd.memset(pairs[:, :, :, :].rearrange("p c e f -> p (c e f)"), -1.0))
            nc.gpsimd.tensor_copy(pairs[:, :, 0:E, 0], cst[:, C_TOK:C_TOK + NC].unsqueeze(2).to_broadcast([P, NC, E])
                                  ).then_inc(pairs_init, 1)
            link(nc.gpsimd.memset(xg[:, :], 0.0))

            def find_slots(e, numbers, done):
                nc.gpsimd.tensor_copy(pair[:, :, 0:5], pairs[:, :, bass.ds(e, 1), 0:5].rearrange("p c e f -> p c (e f)"))
                pl.drain()
                for c in range(NC):
                    last = nc.gpsimd.tensor_scalar(has[:, c, :], numbers, pair[:, c, 4:5].bitcast(F32),
                                                   None, ALU.is_equal)
                last.then_inc(done, 1)

            def store_table(rows, done):
                nc.gpsimd.tensor_tensor(rows, slot_sums[:, :], cst[:, C_OFF:C_OFF + 4], ALU.add)
                pl.drain()
                nc.gpsimd.tensor_tensor(rows[:, 2:3], rows[:, 2:3], rows[:, 3:4], ALU.add).then_inc(done, 1)

            def expert_rows(e):
                return tab[:, bass.ds(e, 1), :].rearrange("p e f -> p (e f)")

            def gather(rows, done):
                nc.gpsimd.tensor_copy(idx_gather[:, 0:1], rows[:, 0:1])
                pl.drain()
                pl.indirect_dma_start(out=xg[:, :], out_offset=None, in_=h_rows,
                                      in_offset=bass.IndirectOffsetOnAxis(ap=idx_gather[:, 0:1], axis=0),
                                      bounds_check=S - 1, oob_is_err=False).then_inc(done, 16)

            def scatter(rows, done):
                nc.gpsimd.tensor_copy(idx_scatter[:, 0:1], rows[:, 1:2])
                pl.drain()
                pl.indirect_dma_start(out=y_rows, out_offset=bass.IndirectOffsetOnAxis(ap=idx_scatter[:, 0:1], axis=0),
                                      in_=y[:, :], in_offset=None,
                                      bounds_check=S * TOPK - 1, oob_is_err=False).then_inc(done, 16)

            def select(tile, column):
                return nc.gpsimd.tensor_copy(tile[:, :], cst[:, bass.ds(C_SEL + column, 1)].to_broadcast([P, P]))

            pl.wait_ge(tab_raw, 1)
            store_table(expert_rows(0), tab_s)
            pl.wait_ge(hn_out, 16 * NC)
            gather(expert_rows(0), gathered)
            select(sel_gu, 0).then_inc(sel_gu_s, 1)
            pl.wait_ge(tab_raw, 2)
            store_table(expert_rows(1), tab_s)
            pl.wait_ge(has_s, 2)
            find_slots(2, slots[:, 0:P], has_s)
            pl.wait_ge(x_tr, 1)
            pl.wait_ge(gathered, 16)
            gather(expert_rows(1), gathered)
            pl.wait_ge(used, U_LOOP)
            select(sel_gu, 1).then_inc(sel_gu_s, 1)
            select(sel_dn, 0).then_inc(sel_dn_s, 1)
            pl.sem_inc(y_free, 1)
            with pl.Fori(0, E - 1) as i:
                pl.wait_ge(x_tr, i + 2)
                pl.wait_ge(gathered, i * 16 + 32)
                pl.wait_ge(tab_raw, i + 3)
                store_table(expert_rows(i + 2), tab_s)
                gather(expert_rows(i + 2), gathered)
                find_slots(i + 3, slots[:, 0:P], has_s)
                pl.wait_ge(used, i * U_E + (U_LOOP + U_GU))
                select(sel_gu, i + 2).then_inc(sel_gu_s, 1)
                pl.wait_ge(used, i * U_E + (U_LOOP + U_E))
                select(sel_dn, i + 1).then_inc(sel_dn_s, 1)
                pl.wait_ge(y_s, i + 2)
                scatter(expert_rows(i), scattered)
                pl.wait_ge(scattered, i * 16 + 16)
                pl.sem_inc(y_free, 1)
            pl.wait_ge(y_s, E + 1)
            scatter(expert_rows(E - 1), scattered)
            pl.wait_ge(scattered, 16 * E)
            pl.wait_ge(x_tr, E + 1)
            pl.wait_ge(gathered, 16 * (E + 1))

            pl.wait_ge(ov_s, 1)
            total = pl.value_load(ov_total[0:1, 0:1], min_val=0, max_val=NOVER)
            with pl.If(total > 0):
                with pl.Fori(0, NOVER) as i:
                    with pl.If(i < total):
                        e = pl.value_load(ov_lists[0:1, 0, bass.ds(i, 1)], min_val=0, max_val=E - 1)
                        first = pl.value_load(ov_lists[0:1, 1, bass.ds(i, 1)], min_val=0, max_val=S - P)
                        select(sel_gu, e).then_inc(v_sel, 1)
                        nc.gpsimd.tensor_copy(slot_row[:, :], slots[:, bass.ds(first, P)])
                        find_slots(e, slot_row[:, :], v_has)
                        pl.wait_ge(v_raw, i + 1)
                        store_table(tab_over[:, :], v_tab)
                        gather(tab_over[:, :], v_gather)
                        pl.wait_ge(v_y, i + 1)
                        nc.gpsimd.tensor_tensor(tab_over[:, 1:2], tab_over[:, 1:2], cst[:, C_OFF + 3:C_OFF + 4], ALU.add)
                        pl.drain()
                        scatter(tab_over[:, :], v_scatter)
                        pl.wait_ge(v_scatter, i * 16 + 16)
            pl.sem_inc(rows_done, 1)
            for c in range(NC):
                pl.wait_ge(picked_in[2 * c], 16)
                nc.gpsimd.tensor_tensor(picked[c][:, 0, :], picked[c][:, 0, :], picked[c][:, 1, :], ALU.add).then_inc(f_pair, 1)

        @block.scalar
        def _(act_e):
            def hi(n, i=0):
                act_e.wait_ge(*full(n, i))
                if n >= SPLIT:
                    act_e.wait_ge(used, i * U_E + (n - SPLIT + 1))
                nc.scalar.activation(whi[:, n % SPLIT, :], raw_slot(slot_of(n)), ACT.Copy).then_inc(hi_done, 1)

            def store_rot(q):
                act_e.wait_ge(rot_tr, q + 1)
                dst = (qT, kT)[(q // NC) % 2]
                c = q % NC
                nc.scalar.activation(dst[:, :, c * P:(c + 1) * P],
                                     ps[:, 4 + q % 2, :].rearrange("p (h t) -> p h t", h=H), ACT.Copy).then_inc(rot_out, 1)

            act_e.dma_start(cst[:, :], small_d).then_inc(cst_in, 16)
            with nc.allow_non_contiguous_dma(reason="1024 gains, one for each feature, onto partitions"):
                act_e.dma_start(gmix[:, :], norm_mix_g[0].rearrange("(k p) -> p k", p=P)).then_inc(gmix_in, 16)
            hi(0)
            act_e.wait_ge(x_in[NC - 1], 16)
            act_e.dma_start(mix[:, :], mix_d).then_inc(mix_in, 16)
            act_e.wait_ge(gmix_in, 16)
            for j in range(KD):
                act_e.wait_ge(xT_tr, j + 1)
                nc.scalar.activation(hT_hi[:, j, :], ps[:, 4 + j % 4, :], ACT.Copy,
                                     scale=gmix[:, j:j + 1]).then_inc(hThi_s, 1)
            hi(1)
            for c in range(NC):
                act_e.wait_ge(x_in[c], 16)
                nc.scalar.activation(squares0[:, c, :], x1[:, c, :], ACT.Square,
                                     accum_out=small[:, 0, c:c + 1]).then_inc(sq, 1)
            act_e.wait_ge(var_s, 1)
            nc.scalar.activation(small[:, 2, 0:NC], small[:, 1, 0:NC], ACT.Sqrt).then_inc(root_s, 1)

            copied = {AV: avt, RG: rgt, RV: rvt}
            n_rot = 0
            for b in range(8 * NG):
                n, c = divmod(b, NC)
                gi, u = divmod(n, 2)
                if c == 0:
                    hi(n + 2)
                if 24 <= b < 24 + NC * H:
                    j = b - 24
                    act_e.wait_ge(a_pv, j + 1)
                    act_e.wait_ge(a_rden, j + 1)
                    nc.scalar.activation(cat_att[:, j % NC, (j // NC) * DH:(j // NC + 1) * DH], ps[:, 7, 0:DH],
                                         ACT.Copy, scale=small[:, 7, j:j + 1]).then_inc(a_out, 1)
                if RET + 2 <= b < RET + 2 + H:
                    act_e.wait_ge(r_pv, b - RET - 1)
                    h = b - RET - 2
                    nc.scalar.activation(cat_ret[:, :, h * DH:(h + 1) * DH],
                                         ps[:, 7, :].rearrange("p (c d) -> p c d", c=NC), ACT.Copy).then_inc(r_copy, 1)
                if u == 1 and GROUPS[gi] in copied:
                    wait_bank(act_e, gi, c)
                    act_e.wait_ge(rstd_s, 1)
                    nc.scalar.activation(copied[GROUPS[gi]][:, c, :], ps[:, c, :], ACT.Copy,
                                         scale=row_rms[:, c:c + 1]).then_inc(drained_s, 1)
                if 20 <= b < 20 + NC * H:
                    j = b - 20
                    kw = (j % NC + 1) * P
                    act_e.wait_ge(a_max, j + 1)
                    nc.scalar.activation(prob[:, j % 3, 0:kw], prob[:, j % 3, 0:kw], ACT.Exp, scale=SCALE,
                                         bias=small[:, 5, j:j + 1]).then_inc(a_exp, 1)
                if 22 <= b < 22 + NC * H:
                    j = b - 22
                    kw = (j % NC + 1) * P
                    act_e.wait_ge(a_tr, j + 1)
                    if j:
                        act_e.wait_ge(a_pv, j)
                    nc.scalar.activation(probT[:, 0:kw], ps[:, 6, 0:kw], ACT.Copy).then_inc(a_pT, 1)
                if u == 1 and GROUPS[gi] == RG:
                    act_e.wait_ge(drained_s, 2 * NC + c + 1)
                    act_e.wait_ge(a_pv, NC * H)
                    if c:
                        act_e.wait_ge(g_use, c)
                    nc.scalar.activation(probT[:, :], rgt[:, c, :], ACT.Sigmoid).then_inc(g_sig, 1)
                rb = b - 2
                if rb >= 0 and (rb // NC) % 2 == 1 and GROUPS[rb // 8] in (AQ, AK, RQ, RK):
                    store_rot(n_rot)
                    n_rot += 1
            for h in range(H):
                act_e.wait_ge(c_tr, h + 1)
                nc.scalar.activation(catT_hi[:, H + h, :], ps[:, 6 + h % 2, :], ACT.Copy).then_inc(c_hi, 1)
            hi(16)
            act_e.wait_ge(gn_var, 1)
            nc.scalar.activation(small[:, 9, :], small[:, 8, :], ACT.Sqrt).then_inc(gn_root, 1)
            for h in range(H):
                act_e.wait_ge(c_tr, H + h + 1)
                nc.scalar.activation(catT_hi[:, h, :], ps[:, 4 + h % 2, :], ACT.Copy).then_inc(c_hi, 1)
            hi(17)
            hi(18)

            def store_residual(t):
                g, c = divmod(t, NC)
                act_e.wait_ge(r_tr, t + 1)
                nc.scalar.activation(rT[:, 4 * g:4 * g + 4, c * P:(c + 1) * P],
                                     ps[:, 4 + t % 2, :].rearrange("p (j t) -> p j t", j=4), ACT.Copy).then_inc(rT_s, 1)

            for t in range(NC):
                store_residual(t)
            hi(19)
            for c in range(NC):
                act_e.wait_ge(x1_s, NC + c + 1)
                if c:
                    act_e.wait_ge(sq, NC + c)
                nc.scalar.activation(squares[:, :], x1[:, c, :], ACT.Square,
                                     accum_out=small[:, 0, c:c + 1]).then_inc(sq, 1)
                store_residual(NC + c)
            act_e.wait_ge(var_s, 2)
            nc.scalar.activation(small[:, 2, 0:NC], small[:, 1, 0:NC], ACT.Sqrt).then_inc(root_s, 1)
            act_e.wait_ge(rstd_s, 2)
            for c in range(NC):
                if c == NC // 2:
                    act_e.wait_ge(top_s, 1)
                    nc.scalar.activation(gates[:, :, :], gates[:, :, :], ACT.Exp).then_inc(gexp_s, 1)
                act_e.wait_ge(hn_gain, c + 1)
                nc.scalar.activation(hn[:, c, :], hn[:, c, :], ACT.Copy, scale=small[:, 3, c:c + 1]).then_inc(hn_s, 1)
            act_e.wait_ge(hn_out, 16 * NC)
            for r in (0, E):
                act_e.dma_start(bias_raw[r:r + E, 0:2 * D], b_gate_up[0]).then_inc(bias_in, 16)
                act_e.dma_start(bias_raw[r:r + E, 2 * D:3 * D], b_down[0]).then_inc(bias_in, 16)

            def sigmoid(hn0, i=0):
                act_e.wait_ge(glu_s, i * 2 + (hn0 + 1))
                if hn0 > 0:
                    act_e.wait_ge(act_s, i * 2 + hn0)
                nc.scalar.activation(sig[:, :], glu[:, :], ACT.Sigmoid, scale=ALPHA).then_inc(sig_s, 1)

            def tokens_hi(e, i=0):
                act_e.wait_ge(x_tr, i + (e + 1))
                nc.scalar.activation(xT_hi[:, :, :].rearrange("p k t -> p (k t)"),
                                     ps[:, 6:8, :].rearrange("p b t -> p (b t)"), ACT.Copy).then_inc(x_hi, 1)

            def features_hi(e, i=0):
                act_e.wait_ge(act_tr, i + (e + 1))
                nc.scalar.activation(actT_hi[:, :, :].rearrange("p k t -> p (k t)"),
                                     ps[:, 6:8, :].rearrange("p b t -> p (b t)"), ACT.Copy).then_inc(aT_hi, 1)

            def gated_rows(column, frees, units):
                act_e.wait_ge(used, units)
                act_e.wait_ge(y_free, frees)
                act_e.wait_ge(tab_s, frees)
                nc.scalar.activation(y[:, :], ps[:, 4:6, :].rearrange("p b t -> p (b t)"), ACT.Copy,
                                     scale=tab[:, bass.ds(column, 1), 2]).then_inc(y_s, 1)

            def copy_table(e, i=0):
                act_e.wait_ge(pair_tr, i + (e + 1))
                if e > 0:
                    act_e.wait_ge(tab_s, i + e)
                nc.scalar.activation(slot_sums[:, :], ps[:, 3, 0:4], ACT.Copy).then_inc(tab_raw, 1)

            act_e.sem_inc(y_s, 1)
            copy_table(0)
            copy_table(1)
            hi(20)
            act_e.wait_ge(bias_in, 64)
            nc.scalar.activation(bias[0:2 * E, :], bias_raw[0:2 * E, :], ACT.Copy).then_inc(bias_hi, 1)
            tokens_hi(0)
            for n in (21, 22, 23, 24, 25):
                hi(n)
            sigmoid(0)
            hi(26)
            hi(27)
            tokens_hi(1)
            hi(28)
            sigmoid(1)
            act_e.dma_start(g_row[:, :], norm_final_g.rearrange("(o d) -> o d", o=1).to_broadcast([P, D])).then_inc(fin_g_in, 16)
            with act_e.Fori(0, E - 1) as i:
                hi(29, i)
                hi(30, i)
                features_hi(0, i)
                copy_table(2, i)
                for n in (31, 32, 33):
                    hi(n, i)
                sigmoid(2, i)
                for n in (34, 35, 36):
                    hi(n, i)
                tokens_hi(2, i)
                hi(37, i)
                sigmoid(3, i)
                for n in (38, 39, 40):
                    hi(n, i)
                gated_rows(i, i + 1, i * U_E + (U_LOOP + U_E))
            features_hi(E - 1)
            hi(U_ALL - 1)
            gated_rows(E - 1, E, U_ALL)

            act_e.wait_ge(ov_s, 1)
            total = act_e.value_load(ov_total[0:1, 0:1], min_val=0, max_val=NOVER)
            with act_e.If(total > 0):
                with act_e.Fori(0, NOVER) as i:
                    with act_e.If(i < total):
                        act_e.wait_ge(v_table, i + 1)
                        nc.scalar.activation(slot_sums[:, :], ps[:, 3, 0:4], ACT.Copy).then_inc(v_raw, 1)
                        for half in range(2):
                            act_e.wait_ge(v_mid, i * 2 + (half + 1))
                            nc.scalar.activation(sig[:, :], glu[:, :], ACT.Sigmoid, scale=ALPHA).then_inc(v_sig, 1)
                        act_e.wait_ge(v_free, i * U_E + (RAW + U_E))
                        act_e.wait_ge(v_tab, i + 1)
                        nc.scalar.activation(y[:, :], ps[:, 4:6, :].rearrange("p b t -> p (b t)"), ACT.Copy,
                                             scale=tab_over[:, 2:3]).then_inc(v_y, 1)

            for c in range(NC):
                act_e.wait_ge(f_sum, c + 1)
                nc.scalar.activation(act[:, :], x1[:, c, :], ACT.Square,
                                     accum_out=small[:, 10, c:c + 1]).then_inc(f_sq, 1)
                act_e.wait_ge(f_var, c + 1)
                nc.scalar.activation(small[:, 12, c:c + 1], small[:, 11, c:c + 1], ACT.Sqrt).then_inc(f_root, 1)

        @block.vector
        def _(v):
            chain = [0]

            def link(ins):
                chain[0] += 1
                ins.then_inc(dve, 1)
                v.wait_ge(dve, chain[0])

            def lo(n, i=0):
                v.wait_ge(hi_done, i * U_E + (n + 1))
                nc.vector.tensor_tensor(wlo[:, n % SPLIT, :], raw_slot(slot_of(n)),
                                        whi[:, n % SPLIT, :].bitcast(F32), ALU.subtract).then_inc(lo_done, 1)

            def inverse_root(var, root, r, t):
                link(nc.vector.reciprocal(r, root))
                link(nc.vector.tensor_tensor(t, r, r, ALU.mult))
                link(nc.vector.tensor_tensor(t, t, var, ALU.mult))
                link(nc.vector.tensor_scalar(t, t, -0.5, 1.5, ALU.mult, ALU.add))
                link(nc.vector.tensor_tensor(r, r, t, ALU.mult))

            lo(0)
            v.wait_ge(gmix_in, 16)
            for j in range(KD):
                v.wait_ge(hThi_s, j + 1)
                nc.vector.scalar_tensor_tensor(out=hT_lo[:, j, :], in0=ps[:, 4 + j % 4, :], scalar=gmix[:, j:j + 1],
                                               in1=hT_hi[:, j, :].bitcast(F32), op0=ALU.mult,
                                               op1=ALU.subtract).then_inc(hTlo_s, 1)
            lo(1)
            v.wait_ge(sq, NC)
            nc.vector.tensor_scalar(small[:, 1, 0:NC], small[:, 0, 0:NC], 1.0 / D, EPS, ALU.mult, ALU.add).then_inc(var_s, 1)
            v.wait_ge(var_s, 1)
            v.wait_ge(root_s, 1)
            inverse_root(small[:, 1, 0:NC], small[:, 2, 0:NC], row_rms[:, :], small[:, 13, 0:NC])
            v.sem_inc(rstd_s, 1)
            v.wait_ge(mix_in, 16)
            angles = mix[:, M_COS:M_COS + 2 * NC * DH].rearrange("p (s c d) -> p s c d", s=2, c=NC)
            for c in range(NC):
                last = nc.vector.tensor_scalar(angles[:, :, c, :], angles[:, :, c, :], row_rms[:, c:c + 1], None, ALU.mult)
            link(last)

            def heads(ap):
                return ap.rearrange("p (h d) -> p h d", h=H)

            def rotate(q, b):
                gi, c = b // 8, b % NC
                cosv = mix[:, M_COS + c * DH:M_COS + (c + 1) * DH].unsqueeze(1)
                sinv = mix[:, M_SIN + c * DH:M_SIN + (c + 1) * DH].unsqueeze(1)
                wait_bank(v, gi, c)
                if q >= 2:
                    v.wait_ge(rot_tr, q - 1)
                src, dst, tmp = heads(ps[:, c, :]), heads(rot[:, q % 2, :]), heads(rtmp[:, :])
                hf = DH // 2
                nc.vector.tensor_tensor(dst, src, cosv.to_broadcast([P, H, DH]), ALU.mult)
                nc.vector.tensor_tensor(tmp[:, :, 0:hf], src[:, :, hf:DH], sinv[:, :, 0:hf].to_broadcast([P, H, hf]), ALU.mult)
                nc.vector.tensor_tensor(tmp[:, :, hf:DH], src[:, :, 0:hf], sinv[:, :, hf:DH].to_broadcast([P, H, hf]),
                                        ALU.mult).then_inc(drained_v, 1)
                v.wait_ge(drained_v, q + 1)
                nc.vector.tensor_tensor(dst, dst, tmp, ALU.add).then_inc(rot_s, 1)
                v.wait_ge(rot_s, q + 1)

            st_off = (0, 512, 896, 1152)
            st_bank = ((4, 0), (5, 0), (6, 0), (6, 256))

            def decayed(h):
                v.wait_ge(r_score, h + 1)
                v.wait_ge(*((dec01_in, 16) if h < 2 else (dec23_in, 16)))
                if h == 0:
                    v.wait_ge(a_tr, NC * H)
                if h == 1:
                    v.wait_ge(rot_tr, 16)
                if h >= 2:
                    v.wait_ge(r_pv, h - 1)
                st = (st0, st1)[h % 2]
                dec = decay01[:, h, :] if h < 2 else decay23[:, h - 2, :]
                for kc in range(NC):
                    bank, off = st_bank[kc]
                    w = S - kc * P
                    last = nc.vector.tensor_tensor(st[:, st_off[kc]:st_off[kc] + w], ps[:, bank, off:off + w],
                                                   dec[:, 0:w], ALU.mult)
                last.then_inc(r_st, 1)

            def head_stats(h):
                v.wait_ge(r_copy, h + 1)
                for c in range(NC):
                    last = nc.vector.bn_stats(stats6[:, h * NC + c, :], cat_ret[:, c, h * DH:(h + 1) * DH])
                link(last)
                for c in range(NC):
                    last = nc.vector.bn_aggr(mv[:, h * NC + c, :], stats6[:, h * NC + c, :])
                link(last)

            n_rot = 0
            v.wait_ge(mix_in, 16)
            for b in range(8 * NG):
                n, c = divmod(b, NC)
                gi, u = divmod(n, 2)
                if c == 0:
                    lo(n + 2)
                if RET + 1 <= b < RET + 1 + H:
                    decayed(b - RET - 1)
                if RET + 3 <= b < RET + 3 + H:
                    head_stats(b - RET - 3)
                if 21 <= b < 21 + NC * H:
                    j = b - 21
                    kw = (j % NC + 1) * P
                    v.wait_ge(a_exp, j + 1)
                    nc.vector.tensor_tensor_reduce(out=prob[:, j % 3, 0:kw], in0=prob[:, j % 3, 0:kw],
                                                   in1=mix[:, M_W + S - kw:M_W + S], scale=1.0, scalar=0.0, op0=ALU.mult,
                                                   op1=ALU.add, accum_out=small[:, 6, j:j + 1]).then_inc(a_prob, 1)
                    v.wait_ge(a_prob, j + 1)
                    nc.vector.reciprocal(small[:, 7, j:j + 1], small[:, 6, j:j + 1]).then_inc(a_rden, 1)
                if 20 <= b < 20 + NC * H:
                    j = b - 20
                    kw = (j % NC + 1) * P
                    v.wait_ge(a_score, j + 1)
                    if j >= 3:
                        v.wait_ge(a_tr, j - 2)
                    nc.vector.tensor_tensor_reduce(out=prob[:, j % 3, 0:kw], in0=ps[:, 4 + j % 2, 0:kw],
                                                   in1=mix[:, M_NEG + S - kw:M_NEG + S], scale=1.0, scalar=-3.0e38,
                                                   op0=ALU.add, op1=ALU.max,
                                                   accum_out=small[:, 4, j:j + 1]).then_inc(a_read, 1)
                    v.wait_ge(a_read, j + 1)
                    nc.vector.tensor_scalar(small[:, 5, j:j + 1], small[:, 4, j:j + 1], -SCALE, None, ALU.mult).then_inc(a_max, 1)
                if u == 1 and GROUPS[gi] in (AQ, AK, RQ, RK):
                    rotate(n_rot, b)
                    n_rot += 1
                if u == 1 and GROUPS[gi] == RG:
                    v.wait_ge(g_sig, c + 1)
                    nc.vector.tensor_tensor(rgt[:, c, :], rgt[:, c, :], probT[:, :], ALU.mult).then_inc(g_use, 1)
            head_stats(H - 1)
            for h in range(H):
                v.wait_ge(c_hi, h + 1)
                nc.vector.tensor_tensor(catT_lo[:, H + h, :], ps[:, 6 + h % 2, :], catT_hi[:, H + h, :].bitcast(F32),
                                        ALU.subtract).then_inc(c_lo, 1)

            nc.vector.tensor_copy(small[:, 14, :], mv[:, :, 0])
            nc.vector.tensor_scalar(small[:, 8, :], mv[:, :, 1], EPS, None, ALU.add).then_inc(gn_var, 1)
            v.wait_ge(gn_var, 1)
            v.wait_ge(gn_root, 1)
            inverse_root(small[:, 8, :], small[:, 9, :], small[:, 15, :], small[:, 13, :])
            v.wait_ge(g_use, NC)
            for h in range(H):
                for c in range(NC):
                    piece = cat_ret[:, c, h * DH:(h + 1) * DH]
                    last = nc.vector.tensor_scalar(piece, piece, small[:, 14, 4 * h + c:4 * h + c + 1],
                                                   small[:, 15, 4 * h + c:4 * h + c + 1], ALU.subtract, ALU.mult)
                link(last)
                piece = cat_ret[:, :, h * DH:(h + 1) * DH]
                nc.vector.tensor_tensor(piece, piece, rgt[:, :, h * DH:(h + 1) * DH], ALU.mult).then_inc(r_cat, 1)
            lo(16)
            for h in range(H):
                v.wait_ge(c_hi, H + h + 1)
                nc.vector.tensor_tensor(catT_lo[:, h, :], ps[:, 4 + h % 2, :], catT_hi[:, h, :].bitcast(F32),
                                        ALU.subtract).then_inc(c_lo, 1)
            lo(17)
            v.wait_ge(router_in, 48)
            nc.vector.tensor_tensor(wr[:, :, :], wr[:, :, :], gffn[:, :].unsqueeze(2).to_broadcast([P, KD, E]),
                                    ALU.mult).then_inc(wr_s, 1)

            def residual(g):
                for c in range(NC):
                    wait_bank(v, NG + g, c)
                    piece = x1[:, c, g * UW:(g + 1) * UW]
                    nc.vector.tensor_tensor(piece, piece, ps[:, c, :], ALU.add).then_inc(x1_s, 1)

            residual(0)
            lo(18)
            lo(19)
            v.wait_ge(logit_s, 1)
            link(nc.vector.tensor_copy(logits[:, :, :].rearrange("p c e -> p (c e)"), ps[:, 6, 0:NC * E]))
            residual(1)

            v.wait_ge(sq, 2 * NC)
            nc.vector.tensor_scalar(small[:, 1, 0:NC], small[:, 0, 0:NC], 1.0 / D, EPS, ALU.mult, ALU.add).then_inc(var_s, 1)
            v.wait_ge(var_s, 2)
            v.wait_ge(root_s, 2)
            inverse_root(small[:, 1, 0:NC], small[:, 2, 0:NC], small[:, 3, 0:NC], small[:, 13, 0:NC])
            v.sem_inc(rstd_s, 1)
            v.wait_ge(logit_s, 2)
            flat = logits[:, :, :].rearrange("p c e -> p (c e)")
            link(nc.vector.tensor_tensor(flat, flat, ps[:, 7, 0:NC * E], ALU.add))
            for c in range(NC):
                last = nc.vector.scalar_tensor_tensor(out=logits[:, c, :], in0=logits[:, c, :],
                                                      scalar=small[:, 3, c:c + 1], in1=br[:, :], op0=ALU.mult, op1=ALU.add)
            link(last)
            for c in range(NC):
                last = nc.vector.max(out=top8[:, c, :], in_=logits[:, c, :])
            link(last)
            for c in range(NC):
                last = nc.vector.max_index(out=idx8[:, c, :], in_max=top8[:, c, :], in_values=logits[:, c, :])
            nc.vector.tensor_tensor(gates[:, :, :], top8[:, :, 0:TOPK], top8[:, :, 0:1].to_broadcast([P, NC, TOPK]),
                                    ALU.subtract).then_inc(top_s, 1)
            link(last)
            link(nc.vector.tensor_copy(idxf[:, :].rearrange("p (c k) -> p c k", c=NC), idx8[:, :, 0:TOPK]))
            link(nc.vector.tensor_tensor(onehot[:, :, :], cst[:, C_IOTA:C_IOTA + E].unsqueeze(1).to_broadcast([P, NC * TOPK, E]),
                                         idxf[:, :].unsqueeze(2).to_broadcast([P, NC * TOPK, E]), ALU.is_equal))
            with nc.allow_low_precision(reason="sums of at most a one are exact"):
                nc.vector.tensor_reduce(out=masks[:, :, :], in_=onehot[:, :, :].rearrange("p (c k) e -> p c e k", c=NC),
                                        op=ALU.add, axis=AX.X).then_inc(mask_s, 1)
            rank_of = onehot[:, :, :].rearrange("p (c k) e -> p c k e", c=NC)
            link(nc.vector.scalar_tensor_tensor(out=pair_rank[:, :, :], in0=rank_of[:, :, 2, :], scalar=2.0,
                                                in1=rank_of[:, :, 1, :], op0=ALU.mult, op1=ALU.add))
            link(nc.vector.scalar_tensor_tensor(out=pair_rank[:, :, :], in0=rank_of[:, :, 3, :], scalar=3.0,
                                                in1=pair_rank[:, :, :], op0=ALU.mult, op1=ALU.add))
            v.wait_ge(pairs_init, 1)
            nc.vector.tensor_tensor(pairs[:, :, 0:E, 1], pair_rank[:, :, :],
                                    cst[:, C_DEST:C_DEST + NC].unsqueeze(2).to_broadcast([P, NC, E]), ALU.add)
            v.wait_ge(gexp_s, 1)
            link(nc.vector.reduce_sum(small[:, 1, 0:NC], gates[:, :, :], axis=AX.X))
            link(nc.vector.reciprocal(small[:, 2, 0:NC], small[:, 1, 0:NC]))
            link(nc.vector.tensor_tensor(gates[:, :, :], gates[:, :, :],
                                         small[:, 2, 0:NC].unsqueeze(2).to_broadcast([P, NC, TOPK]), ALU.mult))
            link(nc.vector.tensor_tensor(prod[:, :, :], onehot[:, :, :],
                                         gates[:, :, :].rearrange("p c k -> p (c k)").unsqueeze(2).to_broadcast([P, NC * TOPK, E]),
                                         ALU.mult))
            link(nc.vector.tensor_reduce(out=pair_gate[:, :, :], in_=prod[:, :, :].rearrange("p (c k) e -> p c e k", c=NC),
                                         op=ALU.add, axis=AX.X))
            link(nc.vector.tensor_copy(pairs[:, :, 0:E, 2].bitcast(F32R), pair_gate[:, :, :]))
            nc.vector.tensor_tensor(pairs[:, :, 0:E, 3], pair_gate[:, :, :], pairs[:, :, 0:E, 2], ALU.subtract)
            v.wait_ge(pos_s, 1)
            link(nc.vector.scalar_tensor_tensor(out=pair_pos[:, :, :], in0=ps[:, 1, 0:NC * E].rearrange("p (c e) -> p c e", c=NC),
                                                scalar=1.0, in1=masks[:, :, :].bitcast(F32), op0=ALU.add, op1=ALU.mult))
            nc.vector.tensor_scalar(pairs[:, :, 0:E, 4], pair_pos[:, :, :], -1.0, None, ALU.add).then_inc(pairs_s, 1)
            v.wait_ge(pairs_s, 1)
            nc.vector.tensor_copy(counts[0:1, :], ps[0:1, 2, 0:E]).then_inc(counts_s, 1)
            v.wait_ge(slots_in, 16)
            for e in range(2):
                if e:
                    v.wait_ge(pair_tr, e)
                link(nc.vector.tensor_copy(pair[:, :, 0:5], pairs[:, :, e, 0:5]))
                for c in range(NC):
                    last = nc.vector.tensor_scalar(has[:, c, :], slots[:, 0:P], pair[:, c, 4:5].bitcast(F32), None, ALU.is_equal)
                last.then_inc(has_s, 1)
            lo(20)

            def gate(hn0, units, i=0):
                half = hn0 % 2
                v.wait_ge(used, units)
                if hn0 > 0:
                    v.wait_ge(act_s, i * 2 + hn0)
                nc.vector.tensor_scalar(glu[:, :], ps[:, 2 * half, :], LIMIT, None, ALU.min).then_inc(glu_s, 1)
                nc.vector.tensor_scalar(lin[:, :], ps[:, 2 * half + 1, :], LIMIT, -LIMIT, ALU.min, ALU.max).then_inc(lin_s, 1)
                v.wait_ge(lin_s, i * 2 + (hn0 + 1))
                v.wait_ge(glu_s, i * 2 + (hn0 + 1))
                nc.vector.scalar_tensor_tensor(out=lin[:, :], in0=lin[:, :], scalar=1.0, in1=glu[:, :], op0=ALU.add,
                                               op1=ALU.mult).then_inc(gated_s, 1)

            def activated(hn0, i=0):
                half = hn0 % 2
                v.wait_ge(gated_s, i * 2 + (hn0 + 1))
                v.wait_ge(sig_s, i * 2 + (hn0 + 1))
                nc.vector.tensor_tensor(act[:, half * UW:(half + 1) * UW], lin[:, :], sig[:, :], ALU.mult).then_inc(act_s, 1)

            def tokens_lo(e, i=0):
                v.wait_ge(x_hi, i + (e + 1))
                nc.vector.tensor_tensor(xT_lo[:, :, :].rearrange("p k t -> p (k t)"),
                                        ps[:, 6:8, :].rearrange("p b t -> p (b t)"),
                                        xT_hi[:, :, :].rearrange("p k t -> p (k t)").bitcast(F32),
                                        ALU.subtract).then_inc(x_lo, 1)

            def features_lo(e, i=0):
                v.wait_ge(aT_hi, i + (e + 1))
                nc.vector.tensor_tensor(actT_lo[:, :, :].rearrange("p k t -> p (k t)"),
                                        ps[:, 6:8, :].rearrange("p b t -> p (b t)"),
                                        actT_hi[:, :, :].rearrange("p k t -> p (k t)").bitcast(F32),
                                        ALU.subtract).then_inc(aT_lo, 1)

            tokens_lo(0)
            v.wait_ge(bias_hi, 1)
            nc.vector.tensor_tensor(bias[E:2 * E, :], bias_raw[E:2 * E, :], bias[E:2 * E, :].bitcast(F32),
                                    ALU.subtract).then_inc(bias_s, 1)
            for n in (21, 22, 23, 24):
                lo(n)
            gate(0, U_MOE + 4)
            lo(25)
            activated(0)
            lo(26)
            lo(27)
            tokens_lo(1)
            lo(28)
            gate(1, U_MOE + 8)
            activated(1)
            with v.Fori(0, E - 1) as i:
                lo(29, i)
                lo(30, i)
                features_lo(0, i)
                lo(31, i)
                lo(32, i)
                gate(2, i * U_E + (U_LOOP + 4), i)
                lo(33, i)
                activated(2, i)
                for n in (34, 35, 36):
                    lo(n, i)
                gate(3, i * U_E + (U_LOOP + 8), i)
                tokens_lo(2, i)
                lo(37, i)
                activated(3, i)
                for n in (38, 39, 40):
                    lo(n, i)
            features_lo(E - 1)
            v.wait_ge(counts_s, 1)
            for k in range(3):
                last = nc.vector.tensor_scalar(ovf[0:1, k * E:(k + 1) * E], counts[0:1, :], float(P * (k + 1)), None, ALU.is_gt)
            link(last)
            link(nc.vector.tensor_tensor_scan(out=ovr[0:1, :], data0=cst[0:1, C_ONE:C_ONE + 3 * E], data1=ovf[0:1, :],
                                              initial=0.0, op0=ALU.mult, op1=ALU.add))
            nc.vector.tensor_copy(ov_total[0:1, 0:1], ovr[0:1, 3 * E - 1:3 * E]).then_inc(total_s, 1)
            v.wait_ge(total_s, 1)
            wide = [1, 16, 3 * E]
            link(nc.vector.tensor_tensor(ovr[0:1, :], ovr[0:1, :], ovf[0:1, :], ALU.mult))
            link(nc.vector.tensor_tensor(ov_eq[0:1, :, :], ovr[0:1, :].unsqueeze(1).to_broadcast(wide),
                                         cst[0:1, C_NUM:C_NUM + 16].unsqueeze(2).to_broadcast(wide), ALU.is_equal))
            for k, col in ((0, C_OVE), (1, C_OVC)):
                for r in range(16):
                    last = nc.vector.tensor_tensor_reduce(out=ovt[0:1, r, :], in0=ov_eq[0:1, r, :], in1=cst[0:1, col:col + 3 * E],
                                                          scale=1.0, scalar=0.0, op0=ALU.mult, op1=ALU.add,
                                                          accum_out=ov_out[0:1, k, r:r + 1])
                link(last)
            nc.vector.tensor_copy(ov_lists[0:1, :, :], ov_out[0:1, :, :]).then_inc(ov_s, 1)

            lo(U_ALL - 1)
            v.wait_ge(act_s, 2 * E)
            v.wait_ge(ov_s, 1)
            total = v.value_load(ov_total[0:1, 0:1], min_val=0, max_val=NOVER)
            v.sem_inc(v_act, 1)
            with v.If(total > 0):
                with v.Fori(0, NOVER) as i:
                    with v.If(i < total):
                        v.wait_ge(v_tr, i * 2 + 1)
                        nc.vector.tensor_copy(xT32[:, :, :].rearrange("p k t -> p (k t)"),
                                              ps[:, 6:8, :].rearrange("p b t -> p (b t)")).then_inc(v_xT, 1)
                        for half in range(2):
                            v.wait_ge(v_act, i * 2 + (half + 1))
                            v.wait_ge(v_free, i * U_E + (RAW + 4 * (half + 1)))
                            nc.vector.tensor_scalar(glu[:, :], ps[:, 2 * half, :], LIMIT, None, ALU.min).then_inc(v_mid, 1)
                            nc.vector.tensor_scalar(lin[:, :], ps[:, 2 * half + 1, :], LIMIT, -LIMIT, ALU.min,
                                                    ALU.max).then_inc(v_chain, 1)
                            v.wait_ge(v_mid, i * 2 + (half + 1))
                            v.wait_ge(v_chain, i * 4 + (2 * half + 1))
                            nc.vector.scalar_tensor_tensor(out=lin[:, :], in0=lin[:, :], scalar=1.0, in1=glu[:, :],
                                                           op0=ALU.add, op1=ALU.mult).then_inc(v_chain, 1)
                            v.wait_ge(v_chain, i * 4 + (2 * half + 2))
                            v.wait_ge(v_sig, i * 2 + (half + 1))
                            nc.vector.tensor_tensor(act[:, half * UW:(half + 1) * UW], lin[:, :], sig[:, :],
                                                    ALU.mult).then_inc(v_act, 1)
                        v.wait_ge(v_tr, i * 2 + 2)
                        nc.vector.tensor_copy(actT32[:, :, :].rearrange("p k t -> p (k t)"),
                                              ps[:, 6:8, :].rearrange("p b t -> p (b t)")).then_inc(v_aT, 1)

            def final_sum(c):
                t = picked[c]
                v.wait_ge(f_pair, c + 1)
                link(nc.vector.tensor_tensor(x1[:, c, :], x1[:, c, :], t[:, 0, :], ALU.add))
                v.wait_ge(picked_in[2 * c + 1], 16)
                link(nc.vector.tensor_tensor(t[:, 2, :], t[:, 2, :], t[:, 3, :], ALU.add))
                nc.vector.tensor_tensor(x1[:, c, :], x1[:, c, :], t[:, 2, :], ALU.add).then_inc(f_sum, 1)
                v.wait_ge(f_sum, c + 1)
                nc.vector.tensor_tensor(t[:, 0, :], x1[:, c, :], g_row[:, :], ALU.mult).then_inc(f_gain, 1)

            def final_norm(c):
                v.wait_ge(f_sq, c + 1)
                nc.vector.tensor_scalar(small[:, 11, c:c + 1], small[:, 10, c:c + 1], 1.0 / D, EPS, ALU.mult,
                                        ALU.add).then_inc(f_var, 1)
                v.wait_ge(f_var, c + 1)
                v.wait_ge(f_root, c + 1)
                inverse_root(small[:, 11, c:c + 1], small[:, 12, c:c + 1], small[:, 3, c:c + 1], small[:, 13, c:c + 1])
                v.wait_ge(f_gain, c + 1)
                nc.vector.tensor_scalar(picked[c][:, 0, :], picked[c][:, 0, :], small[:, 3, c:c + 1], None,
                                        ALU.mult).then_inc(f_out, 1)

            v.wait_ge(fin_g_in, 16)
            final_sum(0)
            for c in range(NC):
                if c + 1 < NC:
                    final_sum(c + 1)
                final_norm(c)

        @block.tensor
        def _(pe):
            mm = nc.tensor.matmul

            def three(out_ap, x_hi_ap, x_lo_ap, w_hi_ap, w_lo_ap, start, stop):
                mm(out_ap, x_hi_ap, w_hi_ap, start=start, stop=False)
                mm(out_ap, x_hi_ap, w_lo_ap, start=False, stop=False)
                return mm(out_ap, x_lo_ap, w_hi_ap, start=False, stop=stop)

            def unit_wait(n, i=0):
                pe.wait_ge(hi_done, i * U_E + (n + 1))
                pe.wait_ge(lo_done, i * U_E + (n + 1))

            def unit_part(n, k):
                return whi[:, n % SPLIT, k * UW:(k + 1) * UW], wlo[:, n % SPLIT, k * UW:(k + 1) * UW]

            pe.wait_ge(cst_in, 16)
            for c in range(NC):
                pe.wait_ge(x_in[c], 16)
            for j in range(KD):
                if j >= 4:
                    pe.wait_ge(hTlo_s, j - 3)
                for c in range(NC):
                    last = nc.tensor.transpose(ps[:, 4 + j % 4, c * P:(c + 1) * P], x1[:, c, j * P:(j + 1) * P], ident)
                last.then_inc(xT_tr, 1)

            drains = []
            for g in GROUPS:
                by_v = g in (AQ, AK, RQ, RK)
                drains.append((drained_v if by_v else drained_s, 4 * sum(s is (drained_v if by_v else drained_s) for s, _ in drains)))

            def project(b):
                n, c = divmod(b, NC)
                gi, u = divmod(n, 2)
                if c == 0:
                    unit_wait(n)
                if b in (0, NC):
                    pe.wait_ge(hTlo_s, KU * (u + 1))
                if u == 0 and gi:
                    s, first = drains[gi - 1]
                    pe.wait_ge(s, first + c + 1)
                for k in range(KU):
                    kk = KU * u + k
                    w_hi_ap, w_lo_ap = unit_part(n, k)
                    last = three(ps[:, c, :], hT_hi[:, kk, c * P:(c + 1) * P], hT_lo[:, kk, c * P:(c + 1) * P],
                                 w_hi_ap, w_lo_ap, kk == 0, kk == KD - 1)
                finish(last, u == 1, c == NC - 1)

            def finish(last, bank_full, unit_done):
                if unit_done:
                    last.then_inc(used, 1)
                elif bank_full:
                    last.then_inc(proj, 1)

            def transpose_rot(q):
                pe.wait_ge(rot_s, q + 1)
                if q >= 2:
                    pe.wait_ge(rot_out, q - 1)
                if q == 8:
                    pe.wait_ge(a_read, NC * H)
                for h in range(H):
                    last = nc.tensor.transpose(ps[:, 4 + q % 2, h * P:(h + 1) * P], rot[:, q % 2, h * DH:(h + 1) * DH], ident)
                last.then_inc(rot_tr, 1)

            def scores(j):
                h, c = divmod(j, NC)
                if j == 0:
                    pe.wait_ge(rot_out, 8)
                if j >= 2:
                    pe.wait_ge(a_read, j - 1)
                mm(ps[:, 4 + j % 2, 0:(c + 1) * P], qT[:, h, c * P:(c + 1) * P], kT[:, h, 0:(c + 1) * P],
                   start=True, stop=True).then_inc(a_score, 1)

            def transpose_prob(j):
                pe.wait_ge(a_prob, j + 1)
                if j:
                    pe.wait_ge(a_pT, j)
                for kc in range(j % NC + 1):
                    last = nc.tensor.transpose(ps[:, 6, kc * P:(kc + 1) * P], prob[:, j % 3, kc * P:(kc + 1) * P], ident)
                last.then_inc(a_tr, 1)

            def values(j):
                h, c = divmod(j, NC)
                pe.wait_ge(a_pT, j + 1)
                if j == 0:
                    pe.wait_ge(drained_s, 4)
                if j:
                    pe.wait_ge(a_out, j)
                for kc in range(c + 1):
                    last = mm(ps[:, 7, 0:DH], probT[:, kc * P:(kc + 1) * P], avt[:, kc, h * DH:(h + 1) * DH],
                              start=(kc == 0), stop=(kc == c))
                last.then_inc(a_pv, 1)

            st_off = (0, 512, 896, 1152)
            st_bank = ((4, 0), (5, 0), (6, 0), (6, 256))

            def ret_scores(h):
                if h == 0:
                    pe.wait_ge(rot_out, 16)
                    pe.wait_ge(a_pT, NC * H)
                else:
                    pe.wait_ge(r_st, h)
                for kc in range(NC):
                    bank, off = st_bank[kc]
                    w = S - kc * P
                    last = mm(ps[:, bank, off:off + w], kT[:, h, kc * P:(kc + 1) * P], qT[:, h, kc * P:S], start=True, stop=True)
                last.then_inc(r_score, 1)

            def ret_values(h):
                pe.wait_ge(r_st, h + 1)
                if h == 0:
                    pe.wait_ge(drained_s, 2 * NC)
                    pe.wait_ge(a_out, NC * H)
                else:
                    pe.wait_ge(r_copy, h)
                st = (st0, st1)[h % 2]
                for qc in range(NC):
                    for kc in range(qc + 1):
                        o = st_off[kc] + (qc - kc) * P
                        last = mm(ps[:, 7, qc * P:(qc + 1) * P], st[:, o:o + P], rvt[:, kc, h * DH:(h + 1) * DH],
                                  start=(kc == 0), stop=(kc == qc))
                last.then_inc(r_pv, 1)

            n_rot = 0
            for b in range(8 * NG):
                project(b)
                step = b - 20
                if 3 <= step < NC * H + 3:
                    values(step - 3)
                if 2 <= step < NC * H + 2:
                    transpose_prob(step - 2)
                if 0 <= step < NC * H:
                    scores(step)
                rb = b - 2
                if rb >= 0 and (rb // NC) % 2 == 1 and GROUPS[rb // 8] in (AQ, AK, RQ, RK):
                    transpose_rot(n_rot)
                    n_rot += 1
                step = b - RET
                if 1 <= step < H + 1:
                    ret_values(step - 1)
                if 0 <= step < H:
                    ret_scores(step)

            def transpose_cat(q):
                src, bank = (cat_att, 6 + q % 2) if q < H else (cat_ret, 4 + q % 2)
                if q in (2, 3, 6, 7):
                    pe.wait_ge(c_lo, q - 1)
                if q == 0:
                    pe.wait_ge(a_out, NC * H)
                    pe.wait_ge(r_st, H)
                if q == 1:
                    pe.wait_ge(r_copy, H)
                if q >= H:
                    pe.wait_ge(r_cat, q - H + 1)
                h = q % H
                for c in range(NC):
                    last = nc.tensor.transpose(ps[:, bank, c * P:(c + 1) * P], src[:, c, h * DH:(h + 1) * DH], ident)
                last.then_inc(c_tr, 1)

            for q in range(H):
                transpose_cat(q)

            def out_project(n, c):
                g, part = divmod(n - U_OUT, 2)
                if c == 0:
                    unit_wait(n)
                if part == 0 and g == 0:
                    pe.wait_ge(drained_s, 2 * NC + c + 1)
                if part == 0 and g == 1:
                    pe.wait_ge(x1_s, c + 1)
                if c == 0:
                    pe.wait_ge(c_lo, H if (part == 0) else 2 * H)
                for k in range(KU):
                    kk = KU * (1 - part) + k
                    w_hi_ap, w_lo_ap = unit_part(n, k)
                    last = three(ps[:, c, :], catT_hi[:, kk, c * P:(c + 1) * P], catT_lo[:, kk, c * P:(c + 1) * P],
                                 w_hi_ap, w_lo_ap, part == 0 and k == 0, part == 1 and k == KU - 1)
                finish(last, part == 1, c == NC - 1)

            for c in range(NC):
                out_project(U_OUT, c)
            for q in range(H, 2 * H):
                transpose_cat(q)

            def transpose_residual(t):
                g, c = divmod(t, NC)
                pe.wait_ge(x1_s, t + 1)
                if t >= 2:
                    pe.wait_ge(rT_s, t - 1)
                for j in range(4):
                    d = (4 * g + j) * P
                    last = nc.tensor.transpose(ps[:, 4 + t % 2, j * P:(j + 1) * P], x1[:, c, d:d + P], ident)
                last.then_inc(r_tr, 1)

            def route(t):
                g, c = divmod(t, NC)
                pe.wait_ge(rT_s, t + 1)
                if t == 0:
                    pe.wait_ge(wr_s, 1)
                for j in range(4 * g, 4 * g + 4):
                    last = mm(ps[:, 6 + g, c * E:(c + 1) * E], rT[:, j, c * P:(c + 1) * P], wr[:, j, :],
                              start=(j == 4 * g), stop=(j == 4 * g + 3))
                if c == NC - 1:
                    last.then_inc(logit_s, 1)

            for c in range(NC):
                out_project(U_OUT + 1, c)
            for c in range(NC):
                out_project(U_OUT + 2, c)
                transpose_residual(c)
                if c:
                    route(c - 1)
            for c in range(NC):
                out_project(U_OUT + 3, c)
                if c:
                    transpose_residual(NC + c - 1)
                if c != 1:
                    route(NC - 1 if c == 0 else NC + c - 2)
            transpose_residual(2 * NC - 1)
            route(2 * NC - 2)
            route(2 * NC - 1)
            pe.wait_ge(mask_s, 1)
            pe.wait_ge(ones_s, 2)
            every = masks[:, :, :].rearrange("p c e -> p (c e)")
            mm(ps[:, 1, 0:NC * E], tri_r[:, :], every, start=True, stop=False)
            for c in range(1, NC):
                last = mm(ps[:, 1, c * E:NC * E], ones_r[:, :], every[:, 0:(NC - c) * E], start=False, stop=(c == NC - 1))
            for c in range(NC):
                last = mm(ps[:, 2, 0:E], ones_r[:, :], masks[:, c, :], start=(c == 0), stop=(c == NC - 1))
            last.then_inc(pos_s, 1)

            def table(e, i=0):
                pe.wait_ge(has_s, i + (e + 1))
                for c in range(NC):
                    last = mm(ps[:, 3, 0:4], has[:, c, :], pair[:, c, 0:4], start=(c == 0), stop=(c == NC - 1))
                last.then_inc(pair_tr, 1)

            def tokens(e, i=0):
                pe.wait_ge(gathered, i * 16 + 16 * (e + 1))
                if e > 1:
                    pe.wait_ge(aT_hi, i + (e - 1))
                    pe.wait_ge(aT_lo, i + (e - 1))
                for j in range(KD):
                    last = nc.tensor.transpose(ps[:, 6 + j // 4, (j % 4) * P:(j % 4 + 1) * P], xg[:, j * P:(j + 1) * P], ident)
                last.then_inc(x_tr, 1)

            def features(e, i=0):
                pe.wait_ge(act_s, i * 2 + 2 * (e + 1))
                pe.wait_ge(x_hi, i + (e + 2))
                pe.wait_ge(x_lo, i + (e + 2))
                for j in range(KD):
                    last = nc.tensor.transpose(ps[:, 6 + j // 4, (j % 4) * P:(j % 4 + 1) * P], act[:, j * P:(j + 1) * P], ident)
                last.then_inc(act_tr, 1)

            def half_matrix(n0, i, bank, sel, b0, x_hi_t, x_lo_t):
                for u in range(2):
                    unit_wait(n0 + u, i)
                    for k in range(KU):
                        kk = KU * u + k
                        w_hi_ap, w_lo_ap = unit_part(n0 + u, k)
                        last = three(ps[:, bank, :], x_hi_t[:, kk, :], x_lo_t[:, kk, :], w_hi_ap, w_lo_ap, kk == 0, False)
                    if u == 1:
                        if n0 == U_MOE:
                            pe.wait_ge(bias_s, 1)
                        last = mm(ps[:, bank, :], sel[0:2 * E, :], bias[0:2 * E, b0:b0 + UW], start=False, stop=True)
                    last.then_inc(used, 1)

            def gate_up(n0, e, i=0):
                pe.wait_ge(sel_gu_s, i + (e + 1))
                pe.wait_ge(x_hi, i + (e + 1))
                pe.wait_ge(x_lo, i + (e + 1))
                for q in range(4):
                    if e > 0 and q % 2 == 0:
                        pe.wait_ge(lin_s, i * 2 + (2 * e + q // 2 - 1))
                    if q == 1 and e > 0:
                        features(e - 1, i)
                        pe.wait_ge(lin_s, i * 2 + 2 * e)
                        table(e + 1, i)
                    if q == 3:
                        pe.wait_ge(tab_raw, i + (e + 2))
                    half_matrix(n0 + 2 * q, i, q, sel_gu, GU_COLS[q] * UW, xT_hi, xT_lo)

            def down(n0, e, i=0):
                pe.wait_ge(sel_dn_s, i + (e + 1))
                pe.wait_ge(aT_hi, i + (e + 1))
                pe.wait_ge(aT_lo, i + (e + 1))
                pe.wait_ge(y_s, i + (e + 1))
                for q in range(2):
                    half_matrix(n0 + 2 * q, i, 4 + q, sel_dn, 2 * D + q * UW, actT_hi, actT_lo)

            table(0)
            pe.wait_ge(tab_raw, 1)
            table(1)
            tokens(0)
            pe.wait_ge(counts_s, 1)
            gate_up(U_MOE, 0)
            pe.wait_ge(x_lo, 1)
            tokens(1)
            with pe.Fori(0, E - 1) as i:
                gate_up(U_LOOP, 1, i)
                tokens(2, i)
                down(U_LOOP + U_GU, 0, i)
            features(E - 1)
            down(U_ALL - U_DN, E - 1)

            for r in range(RAW):
                pe.sem_inc(v_free, 1)
            pe.wait_ge(ov_s, 1)
            total = pe.value_load(ov_total[0:1, 0:1], min_val=0, max_val=NOVER)
            with pe.If(total > 0):
                with pe.Fori(0, NOVER) as i:
                    with pe.If(i < total):
                        def whole_matrix(q, bank, b0, x_t):
                            mm(ps[:, bank, :], sel_gu[0:2 * E, :], bias[0:2 * E, b0:b0 + UW], start=True, stop=False)
                            for u in range(2 * q, 2 * q + 2):
                                pe.wait_ge(v_full[u % RAW], i * (16 * U_E // RAW) + 16 * (u // RAW + 1))
                                for k in range(KU):
                                    kk = KU * (u % 2) + k
                                    last = mm(ps[:, bank, :], x_t[:, kk, :], raw[:, u % RAW, k * UW:(k + 1) * UW],
                                              start=False, stop=(kk == KD - 1))
                                last.then_inc(v_free, 1)

                        pe.wait_ge(v_has, i + 1)
                        for c in range(NC):
                            last = mm(ps[:, 3, 0:4], has[:, c, :], pair[:, c, 0:4], start=(c == 0), stop=(c == NC - 1))
                        last.then_inc(v_table, 1)
                        pe.wait_ge(v_gather, i * 16 + 16)
                        pe.wait_ge(v_sel, i + 1)
                        for j in range(KD):
                            last = nc.tensor.transpose(ps[:, 6 + j // 4, (j % 4) * P:(j % 4 + 1) * P], xg[:, j * P:(j + 1) * P], ident)
                        last.then_inc(v_tr, 1)
                        pe.wait_ge(v_xT, i + 1)
                        pe.wait_ge(v_tab, i + 1)
                        for q in range(4):
                            whole_matrix(q, q, GU_COLS[q] * UW, xT32)
                        pe.wait_ge(v_act, i * 2 + 3)
                        for j in range(KD):
                            last = nc.tensor.transpose(ps[:, 6 + j // 4, (j % 4) * P:(j % 4 + 1) * P], act[:, j * P:(j + 1) * P], ident)
                        last.then_inc(v_tr, 1)
                        pe.wait_ge(v_aT, i + 1)
                        for q in (4, 5):
                            whole_matrix(q, q, 2 * D + (q - 4) * UW, actT32)


_INS = ["x", "norm_mix_g", "w_in", "w_out", "norm_ffn_g", "w_router", "b_router",
        "w_gate_up", "b_gate_up", "w_down", "b_down", "norm_final_g"]


def kernel(**inputs):
    import numpy as _np
    import concourse.bacc as _bacc
    from concourse import mybir as _mybir
    from concourse.bass_utils import run_bass_kernel_spmd as _run

    nc = _bacc.Bacc("TRN2", target_bir_lowering=False, num_devices=1)
    arrays, args = {}, []
    for name in _INS:
        a = _np.ascontiguousarray(inputs[name])
        arrays[f"in_{name}"] = a
        args.append(nc.dram_tensor(f"in_{name}", a.shape, _mybir.dt.from_np(a.dtype), kind="ExternalInput").ap())
    out = nc.dram_tensor("out", (1, S, D), F32, kind="ExternalOutput").ap()
    build(nc, *args, out)
    r = _run(nc, [arrays], core_ids=[0])
    return r.results[0]["out"]
```
